# Optimizing a Trainium2 kernel written in Bass

```python
import math
import jax, jax.numpy as jnp
from jax import lax
import numpy as np

D_MODEL = 1024
BATCH = 1
SEQ = 256
DEPTH = 2

GRID_W = 64
CTX_LEN = 256
N_MIXERS = 3
HEAD_DIM = 64
ROPE_BASE = 10000.0
ROPE_PAIRS_PER_AXIS = HEAD_DIM // 4
Q_BLOCK = 128
NORM_EPS = 1e-6
NEG_INF = -1e30
DIFF_HEADS = D_MODEL // (2 * HEAD_DIM)
NA_HEADS = D_MODEL // HEAD_DIM
NA_KH_MAX = 8
NA_KW = 16
SWA_HEADS = D_MODEL // HEAD_DIM
SWA_KV_HEADS = SWA_HEADS // 4
SWA_WINDOW = 128
D_FF = 2816
CONV_W = 3
N_LAYERS_A = (DEPTH + N_MIXERS - 1) // N_MIXERS
N_LAYERS_B = (DEPTH + N_MIXERS - 2) // N_MIXERS
N_LAYERS_C = (DEPTH + N_MIXERS - 3) // N_MIXERS


def rmsnorm(t, g):
    tf = t.astype(jnp.float32)
    tf = tf * lax.rsqrt(jnp.mean(tf * tf, axis=-1, keepdims=True) + NORM_EPS)
    return tf.astype(t.dtype) * g

def rope_tables(n_tokens, dtype):
    t = jnp.arange(n_tokens, dtype=jnp.int32)
    row = (t // GRID_W).astype(jnp.float32)
    col = (t % GRID_W).astype(jnp.float32)
    inv = ROPE_BASE ** (-jnp.arange(ROPE_PAIRS_PER_AXIS, dtype=jnp.float32) / ROPE_PAIRS_PER_AXIS)
    ar = row[:, None] * inv[None, :]
    ac = col[:, None] * inv[None, :]
    return tuple(a.astype(dtype) for a in (jnp.cos(ar), jnp.sin(ar), jnp.cos(ac), jnp.sin(ac)))

def _rotate(t, cos, sin):
    t1, t2 = jnp.split(t, 2, axis=-1)
    return jnp.concatenate([t1 * cos - t2 * sin, t2 * cos + t1 * sin], axis=-1)

def rope_2d(t, tables):
    cr, sr, cc, sc = (a[None, :, None, :] for a in tables)
    half = HEAD_DIM // 2
    return jnp.concatenate([_rotate(t[..., :half], cr, sr), _rotate(t[..., half:], cc, sc)], axis=-1)

def _to_blocks(t, blk):
    b, s = t.shape[:2]
    return jnp.moveaxis(t.reshape(b, s // blk, blk, *t.shape[2:]), 1, 0)

def _from_blocks(t):
    t = jnp.moveaxis(t, 0, 1)
    return t.reshape(t.shape[0], t.shape[1] * t.shape[2], *t.shape[3:])

def _diff_attend(q, k, v, lam, subln, lam_init):
    s = jnp.einsum('bqhjd,bkhjd->bhjqk', q, k).astype(jnp.float32) * (HEAD_DIM ** -0.5)
    p = jax.nn.softmax(s, axis=-1)
    a = (p[:, :, 0] - lam * p[:, :, 1]).astype(v.dtype)
    o = jnp.einsum('bhqk,bkhe->bqhe', a, v)
    o = rmsnorm(o, subln) * (1.0 - lam_init)
    return o.reshape(o.shape[0], o.shape[1], -1)

def diff_attention(h, hc, wqkv, wo, lam_vecs, subln, layer_idx, tables, need_ctx):
    B, S, _ = h.shape
    H, dh = DIFF_HEADS, HEAD_DIM
    lam_init = 0.8 - 0.6 * math.exp(-0.3 * layer_idx)
    lv = lam_vecs.astype(jnp.float32)
    lam = jnp.exp(jnp.sum(lv[0] * lv[1])) - jnp.exp(jnp.sum(lv[2] * lv[3])) + lam_init

    def proj(t):
        n = t.shape[1]
        q, k, v = jnp.split(t @ wqkv, 3, axis=-1)
        return q.reshape(B, n, 2 * H, dh), k.reshape(B, n, 2 * H, dh), v.reshape(B, n, H, 2 * dh)

    q, k, v = proj(h)
    q, k = rope_2d(q, tables), rope_2d(k, tables)
    qc, kc, vc = proj(hc)
    q = q.reshape(B, S, H, 2, dh)
    k = k.reshape(B, S, H, 2, dh)
    n_ctx = hc.shape[1]
    qc = qc.reshape(B, n_ctx, H, 2, dh)
    kc = kc.reshape(B, n_ctx, H, 2, dh)
    k_all = jnp.concatenate([k, kc], axis=1)
    v_all = jnp.concatenate([v, vc], axis=1)
    y = _from_blocks(lax.map(lambda qb: _diff_attend(qb, k_all, v_all, lam, subln, lam_init),
                             _to_blocks(q, Q_BLOCK))) @ wo
    yc = (_diff_attend(qc, kc, vc, lam, subln, lam_init) @ wo) if need_ctx else None
    return y, yc

def _mha(q, k, v, mask=None, bias=None):
    s = jnp.einsum('bqhd,bkhd->bhqk', q, k).astype(jnp.float32) * (q.shape[-1] ** -0.5)
    if bias is not None:
        s = s + bias
    if mask is not None:
        s = jnp.where(mask, s, NEG_INF)
    p = jax.nn.softmax(s, axis=-1).astype(v.dtype)
    return jnp.einsum('bhqk,bkhd->bqhd', p, v)

def neighbourhood_attention(h, hc, wqkv, wo, rpb, need_ctx):
    B, S, _ = h.shape
    H, dh = NA_HEADS, HEAD_DIM
    rows = S // GRID_W
    kh = min(NA_KH_MAX, rows)
    kw = NA_KW

    def proj(t):
        n = t.shape[1]
        q, k, v = jnp.split(t @ wqkv, 3, axis=-1)
        return q.reshape(B, n, H, dh), k.reshape(B, n, H, dh), v.reshape(B, n, H, dh)

    q, k, v = proj(h)
    qc, kc, vc = proj(hc)
    n_ctx = hc.shape[1]
    kg = k.reshape(B, rows, GRID_W, H, dh)
    vg = v.reshape(B, rows, GRID_W, H, dh)
    col = jnp.arange(GRID_W, dtype=jnp.int32)
    col_start = jnp.clip(col - kw // 2, 0, GRID_W - kw)
    col_ok = (col[None, :] >= col_start[:, None]) & (col[None, :] < col_start[:, None] + kw)
    dx_idx = jnp.clip(col[None, :] - col[:, None], -(kw - 1), kw - 1) + (kw - 1)
    mask = jnp.concatenate(
        [jnp.broadcast_to(col_ok[:, None, :], (GRID_W, kh, GRID_W)).reshape(GRID_W, kh * GRID_W),
         jnp.ones((GRID_W, n_ctx), dtype=bool)], axis=-1)
    rpb32 = rpb.astype(jnp.float32)
    ctx_bias = jnp.zeros((H, GRID_W, n_ctx), jnp.float32)

    def row_block(args):
        r, q_row = args
        rs = jnp.clip(r - kh // 2, 0, rows - kh)
        k_win = lax.dynamic_slice_in_dim(kg, rs, kh, axis=1).reshape(B, kh * GRID_W, H, dh)
        v_win = lax.dynamic_slice_in_dim(vg, rs, kh, axis=1).reshape(B, kh * GRID_W, H, dh)
        dy_idx = rs + jnp.arange(kh, dtype=jnp.int32) - r + (NA_KH_MAX - 1)
        bias = rpb32[:, dy_idx[None, :, None], dx_idx[:, None, :]].reshape(H, GRID_W, kh * GRID_W)
        bias = jnp.concatenate([bias, ctx_bias], axis=-1)
        o = _mha(q_row, jnp.concatenate([k_win, kc], axis=1), jnp.concatenate([v_win, vc], axis=1),
                 mask, bias)
        return o.reshape(B, GRID_W, H * dh)

    q_rows = jnp.moveaxis(q.reshape(B, rows, GRID_W, H, dh), 1, 0)
    y = _from_blocks(lax.map(row_block, (jnp.arange(rows, dtype=jnp.int32), q_rows))) @ wo
    yc = (_mha(qc, kc, vc).reshape(B, n_ctx, H * dh) @ wo) if need_ctx else None
    return y, yc

def _gqa_sink(q, k, v, sink, mask=None):
    s = jnp.einsum('bqkgd,bmkd->bkgqm', q, k).astype(jnp.float32) * (HEAD_DIM ** -0.5)
    if mask is not None:
        s = jnp.where(mask, s, NEG_INF)
    b, kv, g, n, _ = s.shape
    s = jnp.concatenate([s, jnp.broadcast_to(sink[None, :, :, None, None], (b, kv, g, n, 1))], axis=-1)
    p = jax.nn.softmax(s, axis=-1)[..., :-1].astype(v.dtype)
    o = jnp.einsum('bkgqm,bmkd->bqkgd', p, v)
    return o.reshape(b, n, -1)

def window_gqa_sink(h, hc, wqkv, wo, sinks, tables, need_ctx):
    B, S, _ = h.shape
    H, KV, dh = SWA_HEADS, SWA_KV_HEADS, HEAD_DIM
    G = H // KV
    n_ctx = hc.shape[1]

    def proj(t):
        n = t.shape[1]
        q, k, v = jnp.split(t @ wqkv, [H * dh, (H + KV) * dh], axis=-1)
        return q.reshape(B, n, H, dh), k.reshape(B, n, KV, dh), v.reshape(B, n, KV, dh)

    q, k, v = proj(h)
    q, k = rope_2d(q, tables), rope_2d(k, tables)
    q = q.reshape(B, S, KV, G, dh)
    qc, kc, vc = proj(hc)
    qc = qc.reshape(B, n_ctx, KV, G, dh)
    sink = sinks.astype(jnp.float32).reshape(KV, G)

    pad = SWA_WINDOW
    kp = jnp.pad(k, ((0, 0), (pad, pad), (0, 0), (0, 0)))
    vp = jnp.pad(v, ((0, 0), (pad, pad), (0, 0), (0, 0)))
    span = Q_BLOCK + 2 * pad
    qi = jnp.arange(Q_BLOCK, dtype=jnp.int32)
    kj = jnp.arange(span, dtype=jnp.int32)
    band = (kj[None, :] >= qi[:, None]) & (kj[None, :] <= qi[:, None] + 2 * SWA_WINDOW)
    ctx_ok = jnp.ones((Q_BLOCK, n_ctx), dtype=bool)

    def block(args):
        n, q_blk = args
        start = n * Q_BLOCK
        k_loc = lax.dynamic_slice_in_dim(kp, start, span, axis=1)
        v_loc = lax.dynamic_slice_in_dim(vp, start, span, axis=1)
        kpos = start - pad + kj
        valid = band & ((kpos >= 0) & (kpos < S))[None, :]
        mask = jnp.concatenate([valid, ctx_ok], axis=-1)
        return _gqa_sink(q_blk, jnp.concatenate([k_loc, kc], axis=1),
                         jnp.concatenate([v_loc, vc], axis=1), sink, mask)

    nb = S // Q_BLOCK
    y = _from_blocks(lax.map(block, (jnp.arange(nb, dtype=jnp.int32), _to_blocks(q, Q_BLOCK)))) @ wo
    yc = (_gqa_sink(qc, kc, vc, sink) @ wo) if need_ctx else None
    return y, yc

def conv_ffn(t, w_up, w_conv, b_conv, w_down):
    n = t.shape[1]
    u = t @ w_up
    half = CONV_W // 2
    up = jnp.pad(u, ((0, 0), (half, half), (0, 0)))
    acc = b_conv
    for tap in range(CONV_W):
        acc = acc + up[:, tap:tap + n] * w_conv[tap]
    a, g = jnp.split(acc, 2, axis=-1)
    return (jax.nn.silu(g) * a) @ w_down

def first_inputs(seed: int = 0) -> dict:
    key = jax.random.key(seed)
    ks = iter(jax.random.split(key, 32))

    def nrm(shape, scale):
        return jax.random.normal(next(ks), shape, jnp.float32) * scale

    D = D_MODEL
    s = D ** -0.5
    return {
        "x": nrm((BATCH, SEQ, D), 1.0),
        "c": nrm((BATCH, D), 1.0),
        "ctx": nrm((BATCH, CTX_LEN, D), 1.0),
        "c_ctx": nrm((D,), 1.0),
        "ada_w": nrm((DEPTH, D, 6 * D), s),
        "ada_b": nrm((DEPTH, 6 * D), 0.02),
        "norm_mix": 1.0 + nrm((DEPTH, D), 0.05),
        "norm_ffn": 1.0 + nrm((DEPTH, D), 0.05),
        "norm_out": 1.0 + nrm((D,), 0.05),
        "ffn_up": nrm((DEPTH, D, 2 * D_FF), s),
        "ffn_conv": nrm((DEPTH, CONV_W, 2 * D_FF), CONV_W ** -0.5),
        "ffn_conv_b": nrm((DEPTH, 2 * D_FF), 0.02),
        "ffn_down": nrm((DEPTH, D_FF, D), D_FF ** -0.5),
        "a_wqkv": nrm((N_LAYERS_A, D, 3 * D), s),
        "a_wo": nrm((N_LAYERS_A, D, D), s),
        "a_lambda": nrm((N_LAYERS_A, 4, HEAD_DIM), 0.1),
        "a_subln": 1.0 + nrm((N_LAYERS_A, 2 * HEAD_DIM), 0.05),
        "b_wqkv": nrm((N_LAYERS_B, D, 3 * D), s),
        "b_wo": nrm((N_LAYERS_B, D, D), s),
        "b_rpb": nrm((N_LAYERS_B, NA_HEADS, 2 * NA_KH_MAX - 1, 2 * NA_KW - 1), 0.5),
        "c_wqkv": nrm((N_LAYERS_C, D, (SWA_HEADS + 2 * SWA_KV_HEADS) * HEAD_DIM), s),
        "c_wo": nrm((N_LAYERS_C, D, D), s),
        "c_sinks": nrm((N_LAYERS_C, SWA_HEADS), 0.5),
    }

def first_block(x, c, ctx, c_ctx, ada_w, ada_b, norm_mix, norm_ffn, norm_out,
              ffn_up, ffn_conv, ffn_conv_b, ffn_down,
              a_wqkv, a_wo, a_lambda, a_subln,
              b_wqkv, b_wo, b_rpb,
              c_wqkv, c_wo, c_sinks):
    S = x.shape[1]
    tables = rope_tables(S, x.dtype)
    xc = ctx
    silu_c = jax.nn.silu(c)
    silu_cc = jax.nn.silu(c_ctx)
    for i in range(DEPTH):
        need_ctx = i < DEPTH - 1
        kind, j = i % N_MIXERS, i // N_MIXERS
        sh1, sc1, g1, sh2, sc2, g2 = jnp.split((silu_c @ ada_w[i] + ada_b[i])[:, None, :], 6, axis=-1)
        csh1, csc1, cg1, csh2, csc2, cg2 = jnp.split(silu_cc @ ada_w[i] + ada_b[i], 6, axis=-1)
        h = rmsnorm(x, norm_mix[i]) * (1.0 + sc1) + sh1
        hc = rmsnorm(xc, norm_mix[i]) * (1.0 + csc1) + csh1
        if kind == 0:
            y, yc = diff_attention(h, hc, a_wqkv[j], a_wo[j], a_lambda[j], a_subln[j], i, tables, need_ctx)
        elif kind == 1:
            y, yc = neighbourhood_attention(h, hc, b_wqkv[j], b_wo[j], b_rpb[j], need_ctx)
        else:
            y, yc = window_gqa_sink(h, hc, c_wqkv[j], c_wo[j], c_sinks[j], tables, need_ctx)
        x = x + g1 * y
        h2 = rmsnorm(x, norm_ffn[i]) * (1.0 + sc2) + sh2
        x = x + g2 * conv_ffn(h2, ffn_up[i], ffn_conv[i], ffn_conv_b[i], ffn_down[i])
        if need_ctx:
            xc = xc + cg1 * yc
            hc2 = rmsnorm(xc, norm_ffn[i]) * (1.0 + csc2) + csh2
            xc = xc + cg2 * conv_ffn(hc2, ffn_up[i], ffn_conv[i], ffn_conv_b[i], ffn_down[i])
    return rmsnorm(x, norm_out)


N_BRANCH = 4
BRANCH_WIDTH = D_MODEL // N_BRANCH
NSA_HEADS = BRANCH_WIDTH // HEAD_DIM
NSA_CMP_LEN = 32
NSA_CMP_STRIDE = 16
NSA_CMP_HIDDEN = 2 * HEAD_DIM
NSA_SEL_LEN = 64
NSA_N_SEL = 16
NSA_WINDOW = 512
NSA_FORCE_BONUS = 1.0e4
POOL_WINDOWS = (2, 4, 8, 16)
POOL_GROUP = BRANCH_WIDTH // len(POOL_WINDOWS)
CONV_WIDTH = 3
FOX_HEADS = BRANCH_WIDTH // HEAD_DIM
ROPE_THETA = 500000.0
ROPE_DIM = HEAD_DIM // 4
MASK_VALUE = -1e30

IN_SPLITS = (
    NSA_HEADS * HEAD_DIM,
    6 * HEAD_DIM,
    3 * NSA_HEADS,
    BRANCH_WIDTH,
    3 * BRANCH_WIDTH,
    3 * BRANCH_WIDTH,
    FOX_HEADS,
    N_BRANCH * BRANCH_WIDTH,
    N_BRANCH * D_MODEL,
)
D_IN = sum(IN_SPLITS)


def rmsnorm_2(x, g):
    xf = x.astype(jnp.float32)
    y = xf * lax.rsqrt(jnp.mean(xf * xf, axis=-1, keepdims=True) + NORM_EPS)
    return (y * g.astype(jnp.float32)).astype(x.dtype)

def rope(x, pos):
    half = ROPE_DIM // 2
    inv = ROPE_THETA ** (-jnp.arange(half, dtype=jnp.float32) / half)
    ang = pos.astype(jnp.float32)[:, None] * inv[None, :]
    cos = jnp.cos(ang)[None, :, None, :].astype(x.dtype)
    sin = jnp.sin(ang)[None, :, None, :].astype(x.dtype)
    x1, x2, rest = x[..., :half], x[..., half:ROPE_DIM], x[..., ROPE_DIM:]
    return jnp.concatenate([x1 * cos - x2 * sin, x2 * cos + x1 * sin, rest], axis=-1)

def masked_softmax(s, mask):
    s = jnp.where(mask, s.astype(jnp.float32), MASK_VALUE)
    p = jax.nn.softmax(s, axis=-1)
    return jnp.where(mask, p, 0.0)

def to_blocks(a):
    B, T = a.shape[:2]
    a = a.reshape((B, T // Q_BLOCK, Q_BLOCK) + a.shape[2:])
    return jnp.moveaxis(a, 1, 0)

def from_blocks(a):
    a = jnp.moveaxis(a, 0, 1)
    return a.reshape((a.shape[0], a.shape[1] * a.shape[2]) + a.shape[3:])

def nsa_compress(k, pos_emb, w1, b1, w2, b2):
    B, T, hd = k.shape
    nc = (T - NSA_CMP_LEN) // NSA_CMP_STRIDE + 1
    idx = np.arange(nc)[:, None] * NSA_CMP_STRIDE + np.arange(NSA_CMP_LEN)[None, :]
    blocks = k[:, idx] + pos_emb
    flat = blocks.reshape(B, nc, NSA_CMP_LEN * hd)
    return jax.nn.silu(flat @ w1 + b1) @ w2 + b2

def nsa_mixer(q, kv, gate_logits, cmp_pos, cmp_w1, cmp_b1, cmp_w2, cmp_b2):
    B, T = q.shape[:2]
    pos = jnp.arange(T)
    q = rope(q.reshape(B, T, NSA_HEADS, HEAD_DIM), pos) * (HEAD_DIM ** -0.5)
    k_c, v_c, k_s, v_s, k_w, v_w = jnp.split(kv, 6, axis=-1)
    k_s = rope(k_s[:, :, None], pos)[:, :, 0]
    k_w = rope(k_w[:, :, None], pos)[:, :, 0]
    kc = nsa_compress(k_c, cmp_pos[0], cmp_w1[0], cmp_b1[0], cmp_w2[0], cmp_b2[0])
    vc = nsa_compress(v_c, cmp_pos[1], cmp_w1[1], cmp_b1[1], cmp_w2[1], cmp_b2[1])
    nc = kc.shape[1]
    cmp_end_np = np.arange(nc) * NSA_CMP_STRIDE + NSA_CMP_LEN - 1
    cmp_end = jnp.asarray(cmp_end_np)
    kc = rope(kc[:, :, None], cmp_end)[:, :, 0]
    n_blk = T // NSA_SEL_LEN
    n_sel = min(NSA_N_SEL, n_blk)
    ci = np.arange(nc)[:, None] * NSA_CMP_STRIDE
    sj = np.arange(n_blk)[None, :] * NSA_SEL_LEN
    overlap = jnp.asarray((ci < sj + NSA_SEL_LEN) & (ci + NSA_CMP_LEN > sj), jnp.float32)
    k_blk = k_s.reshape(B, n_blk, NSA_SEL_LEN, HEAD_DIM)
    v_blk = v_s.reshape(B, n_blk, NSA_SEL_LEN, HEAD_DIM)
    pad = ((0, 0), (NSA_WINDOW, 0), (0, 0))
    k_wp, v_wp = jnp.pad(k_w, pad), jnp.pad(v_w, pad)
    blk_ids = jnp.arange(n_blk)

    def one_block(args):
        qi, q_blk = args
        t = qi * Q_BLOCK + jnp.arange(Q_BLOCK)
        s = jnp.einsum('bqhd,bnd->bhqn', q_blk, kc)
        p_c = masked_softmax(s, (cmp_end[None, :] <= t[:, None])[None, None])
        o_cmp = jnp.einsum('bhqn,bnd->bqhd', p_c.astype(vc.dtype), vc)
        imp = jnp.einsum('bhqn,nj->bqj', p_c, overlap)
        jt = (t // NSA_SEL_LEN)[:, None]
        j = blk_ids[None, :]
        forced = (j == 0) | (j == jt) | (j == jt - 1)
        valid = j * NSA_SEL_LEN <= t[:, None]
        imp = jnp.where(valid, jnp.where(forced, imp + NSA_FORCE_BONUS, imp), MASK_VALUE)
        _, sel = lax.top_k(imp, n_sel)
        ks = jax.vmap(lambda kb, ib: kb[ib])(k_blk, sel)
        vs = jax.vmap(lambda vb, ib: vb[ib])(v_blk, sel)
        kpos = sel[..., None] * NSA_SEL_LEN + jnp.arange(NSA_SEL_LEN)
        m_s = (kpos <= t[None, :, None, None]).reshape(B, 1, Q_BLOCK, n_sel * NSA_SEL_LEN)
        s = jnp.einsum('bqhd,bqnkd->bhqnk', q_blk, ks).reshape(B, NSA_HEADS, Q_BLOCK, n_sel * NSA_SEL_LEN)
        p_s = masked_softmax(s, m_s).reshape(B, NSA_HEADS, Q_BLOCK, n_sel, NSA_SEL_LEN)
        o_slc = jnp.einsum('bhqnk,bqnkd->bqhd', p_s.astype(vs.dtype), vs)
        kw = lax.dynamic_slice_in_dim(k_wp, qi * Q_BLOCK, Q_BLOCK + NSA_WINDOW, axis=1)
        vw = lax.dynamic_slice_in_dim(v_wp, qi * Q_BLOCK, Q_BLOCK + NSA_WINDOW, axis=1)
        wpos = qi * Q_BLOCK - NSA_WINDOW + jnp.arange(Q_BLOCK + NSA_WINDOW)
        m_w = (wpos[None, :] <= t[:, None]) & (wpos[None, :] > t[:, None] - NSA_WINDOW) & (wpos[None, :] >= 0)
        s = jnp.einsum('bqhd,bkd->bhqk', q_blk, kw)
        p_w = masked_softmax(s, m_w[None, None])
        o_win = jnp.einsum('bhqk,bkd->bqhd', p_w.astype(vw.dtype), vw)
        return o_cmp, o_slc, o_win

    o_cmp, o_slc, o_win = lax.map(one_block, (jnp.arange(T // Q_BLOCK), to_blocks(q)))
    g = jax.nn.sigmoid(gate_logits.reshape(B, T, 3, NSA_HEADS))[..., None]
    o = (g[:, :, 0] * from_blocks(o_cmp) + g[:, :, 1] * from_blocks(o_slc)
         + g[:, :, 2] * from_blocks(o_win))
    return o.reshape(B, T, NSA_HEADS * HEAD_DIM)

def pool_mixer(u, pool_w, pool_scale):
    B, T, C = u.shape
    cs = jnp.concatenate([jnp.zeros((B, 1, C), jnp.float32),
                          jnp.cumsum(u.astype(jnp.float32), axis=1)], axis=1)
    outs = []
    for gi, w in enumerate(POOL_WINDOWS):
        sl = slice(gi * POOL_GROUP, (gi + 1) * POOL_GROUP)
        csg = cs[..., sl]
        lag = jnp.concatenate([jnp.zeros((B, w - 1, POOL_GROUP), jnp.float32),
                               csg[:, :T + 1 - w]], axis=1)
        cnt = jnp.minimum(jnp.arange(1, T + 1), w).astype(jnp.float32)[None, :, None]
        outs.append(((csg[:, 1:] - lag) / cnt).astype(u.dtype) - u[..., sl])
    pooled = jnp.stack(outs, axis=2)
    mixed = jnp.einsum('btgc,gcd->btgd', pooled, pool_w).reshape(B, T, C)
    return mixed * pool_scale

def conv_mixer(xin, b_gate, c_gate, conv_w):
    T = xin.shape[1]
    u = jnp.pad(c_gate * xin, ((0, 0), (CONV_WIDTH - 1, 0), (0, 0)))
    y = sum(u[:, k:k + T] * conv_w[k] for k in range(CONV_WIDTH))
    return b_gate * y

def fox_mixer(q, k, v, f_logit, f_bias):
    B, T = q.shape[:2]
    q = q.reshape(B, T, FOX_HEADS, HEAD_DIM) * (HEAD_DIM ** -0.5)
    k = k.reshape(B, T, FOX_HEADS, HEAD_DIM)
    v = v.reshape(B, T, FOX_HEADS, HEAD_DIM)
    logf = jax.nn.log_sigmoid(f_logit.astype(jnp.float32) + f_bias.astype(jnp.float32))
    c = jnp.cumsum(logf, axis=1)
    c_keys = jnp.transpose(c, (0, 2, 1))
    kpos = jnp.arange(T)

    def one_block(args):
        qi, q_blk, c_blk = args
        t = qi * Q_BLOCK + jnp.arange(Q_BLOCK)
        s = jnp.einsum('bqhd,bkhd->bhqk', q_blk, k).astype(jnp.float32)
        s = s + jnp.transpose(c_blk, (0, 2, 1))[..., None] - c_keys[:, :, None, :]
        p = masked_softmax(s, (kpos[None, :] <= t[:, None])[None, None])
        return jnp.einsum('bhqk,bkhd->bqhd', p.astype(v.dtype), v)

    o = lax.map(one_block, (jnp.arange(T // Q_BLOCK), to_blocks(q), to_blocks(c)))
    return from_blocks(o).reshape(B, T, FOX_HEADS * HEAD_DIM)

def hybrid_layer(x, norm_g, w_in, fox_f_bias, cmp_pos, cmp_w1, cmp_b1, cmp_w2, cmp_b2,
                 pool_w, pool_scale, conv_w, w_branch, w_out):
    B, T, _ = x.shape
    h = rmsnorm_2(x, norm_g)
    proj = h @ w_in
    split_at = np.cumsum(IN_SPLITS)[:-1].tolist()
    (nsa_q, nsa_kv, nsa_g, pool_in, conv_in, fox_qkv, fox_f,
     gate_in, merge_in) = jnp.split(proj, split_at, axis=-1)
    o_nsa = nsa_mixer(nsa_q, nsa_kv, nsa_g, cmp_pos, cmp_w1, cmp_b1, cmp_w2, cmp_b2)
    o_pool = pool_mixer(pool_in, pool_w, pool_scale)
    c_x, c_b, c_c = jnp.split(conv_in, 3, axis=-1)
    o_conv = conv_mixer(c_x, c_b, c_c, conv_w)
    f_q, f_k, f_v = jnp.split(fox_qkv, 3, axis=-1)
    o_fox = fox_mixer(f_q, f_k, f_v, fox_f, fox_f_bias)
    gates = gate_in.reshape(B, T, N_BRANCH, BRANCH_WIDTH)
    merge = merge_in.reshape(B, T, N_BRANCH, D_MODEL)
    acc = None
    for i, o in enumerate((o_nsa, o_pool, o_conv, o_fox)):
        branch = (o * jax.nn.silu(gates[:, :, i])) @ w_branch[i]
        term = jax.nn.sigmoid(merge[:, :, i]) * branch
        acc = term if acc is None else acc + term
    return x + acc @ w_out

def second_inputs(seed: int = 0) -> dict:
    key = jax.random.key(seed)
    ks = jax.random.split(key, 20)
    f32 = jnp.float32
    nrm = lambda k, shape, scale: jax.random.normal(k, shape, f32) * scale
    cmp_in = NSA_CMP_LEN * HEAD_DIM
    return {
        "x": nrm(ks[0], (BATCH, SEQ, D_MODEL), 1.0),
        "norm_g": 1.0 + nrm(ks[1], (DEPTH, D_MODEL), 0.05),
        "w_in": nrm(ks[2], (DEPTH, D_MODEL, D_IN), D_MODEL ** -0.5),
        "fox_f_bias": 3.0 + nrm(ks[3], (DEPTH, FOX_HEADS), 0.5),
        "cmp_pos": nrm(ks[4], (DEPTH, 2, NSA_CMP_LEN, HEAD_DIM), 0.1),
        "cmp_w1": nrm(ks[5], (DEPTH, 2, cmp_in, NSA_CMP_HIDDEN), cmp_in ** -0.5),
        "cmp_b1": nrm(ks[6], (DEPTH, 2, NSA_CMP_HIDDEN), 0.02),
        "cmp_w2": nrm(ks[7], (DEPTH, 2, NSA_CMP_HIDDEN, HEAD_DIM), NSA_CMP_HIDDEN ** -0.5),
        "cmp_b2": nrm(ks[8], (DEPTH, 2, HEAD_DIM), 0.02),
        "pool_w": nrm(ks[9], (DEPTH, len(POOL_WINDOWS), POOL_GROUP, POOL_GROUP), POOL_GROUP ** -0.5),
        "pool_scale": 1.0 + nrm(ks[10], (DEPTH, BRANCH_WIDTH), 0.1),
        "conv_w": nrm(ks[11], (DEPTH, CONV_WIDTH, BRANCH_WIDTH), CONV_WIDTH ** -0.5),
        "w_branch": nrm(ks[12], (DEPTH, N_BRANCH, BRANCH_WIDTH, D_MODEL), BRANCH_WIDTH ** -0.5),
        "w_out": nrm(ks[13], (DEPTH, D_MODEL, D_MODEL), D_MODEL ** -0.5),
        "final_norm_g": 1.0 + nrm(ks[14], (D_MODEL,), 0.05),
    }

def second_block(x, norm_g, w_in, fox_f_bias, cmp_pos, cmp_w1, cmp_b1, cmp_w2, cmp_b2,
              pool_w, pool_scale, conv_w, w_branch, w_out, final_norm_g):
    for l in range(DEPTH):
        x = hybrid_layer(x, norm_g[l], w_in[l], fox_f_bias[l], cmp_pos[l], cmp_w1[l],
                         cmp_b1[l], cmp_w2[l], cmp_b2[l], pool_w[l], pool_scale[l],
                         conv_w[l], w_branch[l], w_out[l])
    return rmsnorm_2(x, final_norm_g)


def setup_inputs(seed=0):
    out = dict(first_inputs(seed))
    for name, value in second_inputs(seed + 1).items():
        if name != "x":
            out[name + "_2"] = value
    return out


def reference(
    x, c, ctx, c_ctx, ada_w, ada_b, norm_mix, norm_ffn, norm_out, ffn_up, ffn_conv, ffn_conv_b,
    ffn_down, a_wqkv, a_wo, a_lambda, a_subln, b_wqkv, b_wo, b_rpb, c_wqkv, c_wo, c_sinks,
    norm_g_2, w_in_2, fox_f_bias_2, cmp_pos_2, cmp_w1_2, cmp_b1_2, cmp_w2_2, cmp_b2_2, pool_w_2,
    pool_scale_2, conv_w_2, w_branch_2, w_out_2, final_norm_g_2,
):
    x = first_block(
        x, c, ctx, c_ctx, ada_w, ada_b, norm_mix, norm_ffn, norm_out, ffn_up, ffn_conv,
        ffn_conv_b, ffn_down, a_wqkv, a_wo, a_lambda, a_subln, b_wqkv, b_wo, b_rpb, c_wqkv,
        c_wo, c_sinks,
    )
    return second_block(
        x, norm_g_2, w_in_2, fox_f_bias_2, cmp_pos_2, cmp_w1_2, cmp_b1_2, cmp_w2_2, cmp_b2_2,
        pool_w_2, pool_scale_2, conv_w_2, w_branch_2, w_out_2, final_norm_g_2,
    )


_drawn_inputs = setup_inputs


def setup_inputs(seed=0):
    import zlib

    import numpy as np

    out = dict(_drawn_inputs(seed))
    spreads = {}
    factors = {'cmp_pos_2': 4.752, 'cmp_b1_2': 23.454, 'cmp_b2_2': 8.0}
    for name, (base, spread) in spreads.items():
        noise = np.random.default_rng([zlib.crc32(name.encode()), seed]).standard_normal(out[name].shape)
        drawn = base * np.exp(spread * noise) if base else spread * noise
        out[name] = __import__('jax').numpy.asarray(drawn.astype(out[name].dtype))
    for name, factor in factors.items():
        out[name] = (out[name] * factor).astype(out[name].dtype)
    return out
```

```python
from collections import deque
from contextlib import ExitStack

import concourse.bass as bass
import numpy as np
from concourse import mybir

F32 = mybir.dt.float32
F32R = mybir.dt.float32r
ALU = mybir.AluOpType
ACT = mybir.ActivationFunctionType
AX = mybir.AxisListType.X

P = 128
D = 1024
DT = 8
FF = 2816
FT = 22
HALF_FT = 11
EPS = 1e-6
NEG = -1e30
LAM_INIT = 0.8 - 0.6 * float(np.exp(-0.3 * 0))

RAW_SLOTS = 3
SPLIT_SLOTS = 3
LOOK = 2
UNIT = 2048
N_TMP = 10
BRANCHES = ("nsa", "pool", "conv", "fox")



def unit_keys():
    keys = []
    for l in range(2):
        keys += [("ada", l, g, half) for g in range(12) for half in range(2)]
        keys += [("qkv", l, i) for i in range(12)]
        keys += [("wo", l, i) for i in range(4)]
        keys += [("up", l, j) for j in range(FT)]
        keys += [("down", l, c, m) for c in range(2) for m in range(DT)]
        keys += [("in", l, i) for i in range(31)]
        keys += [("cmp", l, i) for i in range(2)]
        keys += [("br", l, i) for i in range(4)]
        keys += [("out", l, i) for i in range(4)]
    return keys


KEYS = unit_keys()
UNIT_OF = {k: n for n, k in enumerate(KEYS)}


def in_columns(i):
    r = lambda a, n: list(range(a, a + n))
    if i == 0:
        return r(0, 256)
    if i == 1:
        return r(384, 64) * 2 + r(512, 64) * 2
    if i == 2:
        return r(256, 64) * 2 + r(320, 64) * 2
    if i == 3:
        return r(448, 64) + r(576, 64) + r(640, 12) + r(2444, 4) + [-1] * 112
    if i == 4:
        return r(2188, 256)
    if i == 5:
        return r(1676, 256)
    if i == 6:
        return r(1932, 256)
    if i == 7:
        return r(652, 256)
    if i <= 10:
        return r(908 + 256 * (i - 8), 256)
    if i <= 14:
        return r(2448 + 256 * (i - 11), 256)
    return r(3472 + 256 * (i - 15), 256)




def small_plan():
    at, n = {}, 0
    for name, w in (
        ("c", 8), ("cc", 8), ("adab", 96), ("nmix", 16), ("nffn", 16), ("nout", 8), ("fconv", 264), ("fconvb", 88),
        ("subln", 1), ("normg", 16), ("foxb", 8), ("cpos", 64), ("cb1", 4), ("cb2", 2), ("pscale", 4), ("cw", 12),
        ("fng", 8), ("lam", 256),
    ):
        at[name] = n
        n += w
    return at, n


SM, NSM = small_plan()


def const_plan():
    at, n = {}, 0
    for name, w in (
        ("ident", 128), ("ones", 256), ("c1", 256), ("s1", 256), ("cmpc", 16), ("cmps", 16), ("mna", 64),
        ("cmpadd", 32), ("cmpmul", 32), ("sel", 2), ("mhalf", 1),
    ):
        at[name] = n
        n += w
    return at, n


CO, NCO = const_plan()

LATE = {"c2": 0, "s2": 256, "causal": 512, "icnt": 640, "cb2v": 1152, "poolw": 1280, "w2": 1792}
NLATE = 2304


def constants():
    c = np.zeros((P, NCO), np.float32)
    late = np.zeros((P, NLATE), np.float32)
    p = np.arange(P)
    t = np.arange(256)
    f = np.float32

    def put(name, a):
        a = np.asarray(a, np.float32)
        to, at = (late, LATE) if name in LATE else (c, CO)
        to[:, at[name]:at[name] + a.shape[1]] = a

    put("ident", np.eye(P))
    put("ones", np.ones((P, 256)))
    inv = f(10000.0) ** (-np.arange(16, dtype=f) / f(16))
    row, col = (t // 64).astype(f), (t % 64).astype(f)
    d = p % 64
    pos = np.where((d < 32)[:, None], row[None, :], col[None, :]).astype(f)
    ang = (pos * inv[d % 16][:, None]).astype(f)
    sign = np.where(d % 32 < 16, f(-1), f(1))[:, None]
    put("c1", np.cos(ang))
    put("s1", np.sin(ang) * sign)
    inv2 = f(500000.0) ** (-np.arange(8, dtype=f) / f(8))
    sign2 = np.where(d % 16 < 8, f(-1), f(1))[:, None]
    for names, ps in ((("c2", "s2"), t.astype(f)), (("cmpc", "cmps"), (np.arange(16) * 16 + 31).astype(f))):
        a2 = (ps[None, :] * inv2[d % 8][:, None]).astype(f)
        on = (d < 16)[:, None]
        put(names[0], np.where(on, np.cos(a2), 1.0))
        put(names[1], np.where(on, np.sin(a2) * sign2, 0.0))
    put("causal", np.where(p[None, :] <= p[:, None], 0.0, NEG))
    cc = p % 64
    cs = np.clip(cc - 8, 0, 48)
    k = np.arange(64)
    put("mna", np.where((k[None, :] >= cs[:, None]) & (k[None, :] < cs[:, None] + 16), 0.0, NEG))
    n = np.arange(16)
    ok = np.stack([(n[None, :] * 16 + 31 <= (q * 128 + p)[:, None]) & (n < 15)[None, :] for q in range(2)], 1)
    put("cmpadd", np.where(ok, 0.0, NEG).reshape(P, 32))
    put("cmpmul", ok.reshape(P, 32))
    w = np.stack([np.where(p < 64, 2, 4), np.where(p < 64, 8, 16)], 1)
    put("icnt", (f(1) / np.minimum(t[None, None, :] + 1, w[:, :, None]).astype(f)).reshape(P, 512))
    sel = np.zeros((P, 2))
    sel[[0, 2], 0] = 1
    sel[[1, 3], 1] = 1
    put("sel", sel)
    put("mhalf", np.full((P, 1), -0.5))
    return c, late




class Lane:

    def __init__(self, sem):
        self.sem, self.n, self.queue = sem, 0, []

    def __call__(self, fn, *waits):
        self.n += 1
        self.queue.append((waits, fn, self.sem, 1))
        return (self.sem, self.n)

    def quiet(self, fn, *waits):
        self.queue.append((waits, fn, None, 0))

    def wait_for(self, tokens):
        self.queue.append(((tokens,), None, None, 0))

    def dma(self, fn, counter, *waits):
        counter[1] += 16
        self.queue.append((waits, fn, counter[0], 16))
        return (counter[0], counter[1])

    def play(self, eng):
        seen = {}

        def wait(w):
            if w is None:
                return
            if isinstance(w, list):
                for x in w:
                    wait(x)
                return
            s, v = w
            if seen.get(s.name, 0) < v:
                eng.wait_ge(s, v)
                seen[s.name] = v

        for waits, fn, sem, n in self.queue:
            wait(list(waits))
            if fn is None:
                continue
            ins = fn(eng)
            if sem is not None:
                ins.then_inc(sem, n)


class Pool:

    def __init__(self, items):
        self.free = deque((x, []) for x in items)

    def take(self):
        return self.free.popleft()

    def give(self, item, *tokens):
        self.free.append((item, list(tokens)))


def bass_two_block_decoder(nc, wstream, small, consts, late, rpb, xin, out):
    ctx = ExitStack()
    with ctx:
        def sb(name, shape, dt=F32, stack=ctx):
            return stack.enter_context(nc.sbuf_tensor(name, shape, dt))

        def new_sem(name):
            return ctx.enter_context(nc.semaphore(name))

        sp, act, dve, pool, pe = (Lane(new_sem(f"s_{n}")) for n in ("sp", "act", "dve", "pool", "pe"))
        d_small, d_const, d_out = ([new_sem(n), 0] for n in ("d_small", "d_const", "d_out"))
        d_late = [new_sem("d_late"), 0]
        d_x = [[new_sem(f"d_x{m}"), 0] for m in range(2)]
        d_raw = [[new_sem(f"d_raw{i}"), 0] for i in range(RAW_SLOTS)]
        d_bias = [[new_sem(f"d_bias{i}"), 0] for i in range(2)]

        banks = Pool([ctx.enter_context(nc.psum_tensor(f"ps{i}", [P, 512], F32)) for i in range(8)])
        SMALL = sb("SMALL", [P, NSM])
        CONST = sb("CONST", [P, NCO])
        X = sb("X", [P, DT, 512])
        RAW = sb("RAW", [P, RAW_SLOTS, UNIT])
        WH = sb("WH", [P, SPLIT_SLOTS, UNIT], F32R)
        WL = sb("WL", [P, SPLIT_SLOTS, UNIT], F32R)
        NH = sb("NH", [P, DT, 512], F32R)
        NL = sb("NL", [P, DT, 512], F32R)
        TMP = sb("TMP", [P, N_TMP, 512])
        CB = sb("CB", [P, 160], F32R)
        CS = sb("CS", [P, 32])
        ADA = sb("ADA", [P, 2, 48, 2])
        AMOD = sb("AMOD", [P, 2, 2, 8, 2])
        MS = sb("MS", [P, 8])
        RS = sb("RS", [P, 8])
        STAT = sb("STAT", [P, 8, 32])
        LAMV = sb("LAMV", [P, 8])
        late_sb = [None]
        tmps = Pool(list(range(N_TMP)))
        stats = Pool(list(range(8)))

        def small_at(name, a, n=1):
            if name in LATE:
                return late_sb[0][:, LATE[name] + a:LATE[name] + a + n]
            return SMALL[:, SM[name] + a:SM[name] + a + n]

        def const_at(name, a=0, n=1):
            if name in LATE:
                return late_sb[0][:, LATE[name] + a:LATE[name] + a + n]
            return CONST[:, CO[name] + a:CO[name] + a + n]

        IDENT = const_at("ident", 0, 128)
        ONE = const_at("ones", 0, 1)

        t_small = sp.dma(lambda e: e.dma_start(SMALL[:, :], small), d_small)
        t_const = sp.dma(lambda e: e.dma_start(CONST[:, :], consts), d_const)
        t_x = [sp.dma(lambda e, a=a: e.dma_start(X[:, 4 * a:4 * a + 4, :], xin[:, 4 * a:4 * a + 4, :]), d_x[a])
               for a in range(2)]

        def new_scope():
            before = [(q.sem, q.n) for q in (act, dve, pool, pe)]
            for q in (act, dve, pool):
                q.wait_for(before)

        def copy_a(o, i, *w, scale=1.0):
            return act(lambda e: e.activation(o, i, ACT.Copy, scale=scale), *w)

        def activ(o, i, func, *w, **kw):
            return act(lambda e: e.activation(o, i, func, **kw), *w)

        def reduce(o, i, op, negate, *w):
            return dve(lambda e: e.tensor_reduce(o, i, AX, op, negate=negate), *w)

        def recip(o, i, *w):
            return dve(lambda e: e.reciprocal(o, i), *w)

        def zero(o, *w):
            o = o.bitcast(mybir.dt.uint32)
            return dve(lambda e: e.memset(o, 0), *w)

        def zero_p(o, *w):
            return pool(lambda e: e.memset(o, 0.0), *w)

        def scan_sum(o, ones, i, *w):
            return dve(lambda e: e.tensor_tensor_scan(o, ones, i, 0.0, ALU.mult, ALU.add), *w)

        def shuffle(o, i, hop, *w):
            return dve(lambda e: e.stream_shuffle(o, i, hop), *w)

        def copy_v(o, i, *w):
            return dve(lambda e: e.tensor_copy(o, i), *w)

        def tt(lane, o, a, b, op, *w):
            return lane(lambda e: e.tensor_tensor(o, a, b, op), *w)

        def ts(o, a, s1, s2, op0, op1, *w):
            if s2 is None:
                return dve(lambda e: e.tensor_scalar(o, a, s1, None, op0), *w)
            return dve(lambda e: e.tensor_scalar(o, a, s1, s2, op0, op1), *w)

        def stt(o, a, s, b, op0, op1, *w):
            return dve(lambda e: e.scalar_tensor_tensor(out=o, in0=a, scalar=s, in1=b, op0=op0, op1=op1), *w)

        def mm(o, l, r, start, stop, *w, signal=False, loose=False):
            fn = lambda e: e.matmul(o, l, r, start=start, stop=stop, skip_group_check=loose)
            return pe(fn, *w) if signal else pe.quiet(fn, *w)

        def mm3(o, lh, ll, rh, rl, start, stop, *w, signal=False):
            mm(o, lh, rh, start, False, *w)
            mm(o, lh, rl, False, False)
            return mm(o, ll, rh, False, stop, signal=signal)

        def tr(o, i, *w, signal=False):
            fn = lambda e: e.transpose(o, i, IDENT)
            return pe(fn, *w) if signal else pe.quiet(fn, *w)

        class Weights:
            def __init__(self):
                self.keys, self.low, self.used, self.made = [], [], [], 0
                self.high = []
                for _ in range(LOOK):
                    self.prepare()

            def prepare(self):
                v = self.made
                if v >= len(KEYS):
                    return
                self.made += 1
                loaded = (d_raw[v % RAW_SLOTS][0], 16 * (v // RAW_SLOTS + 1))
                last_use = self.used[v - SPLIT_SLOTS] if v >= SPLIT_SLOTS else None
                raw = RAW[:, v % RAW_SLOTS, :]
                s = v % SPLIT_SLOTS
                size = lambda: 1408 if self.keys[v][0] == "down" else 8 * 144 if self.keys[v][0::2] == ("in", 3) else UNIT
                self.high.append(act(
                    lambda e: e.activation(WH[:, s, 0:size()], raw[:, 0:size()], ACT.Copy), loaded, last_use))
                lane = pool if v % 4 == 1 else dve
                self.low.append(lane(
                    lambda e: e.tensor_tensor(WL[:, s, 0:size()], raw[:, 0:size()],
                                              WH[:, s, 0:size()].bitcast(F32), ALU.subtract),
                    self.high[v]))

            def take(self, key, nk, nc_):
                v = len(self.keys)
                self.keys.append(key)
                self.prepare()
                s = v % SPLIT_SLOTS
                view = lambda t: t[:, s, 0:nk * nc_].rearrange("p (k n) -> p k n", k=nk)
                return view(WH), view(WL), [self.high[v], self.low[v]]

            def done(self, token):
                self.used.append(token)

            def loads(self):
                for v, key in enumerate(self.keys):
                    n = UNIT_OF[key]
                    free = self.low[v - RAW_SLOTS] if v >= RAW_SLOTS else None
                    size = 1408 if key[0] == "down" else 8 * 144 if key[0::2] == ("in", 3) else UNIT
                    sp.dma(lambda e, v=v, n=n, size=size: e.dma_start(
                        RAW[:, v % RAW_SLOTS, 0:size], wstream[n, :, 0:size]), d_raw[v % RAW_SLOTS], free)

        t = zero(CB[:, 32:160])
        t_cb0 = t
        cs = CS[:, 0:16]
        t = activ(cs, small_at("c", 0, 16), ACT.Silu, t_small)
        csv = cs.rearrange("p (v k) -> p k v", v=2)
        cbv = CB[:, 0:32].rearrange("p (k s v) -> p k s v", k=8, s=2)
        t1 = copy_v(cbv[:, :, 0, :], csv, t)
        t_cb = [t_cb0, tt(dve, cbv[:, :, 1, :], csv, cbv[:, :, 0, :].bitcast(F32), ALU.subtract, t1)]

        W = Weights()
        pending = []
        t_ada = {}

        def ada_group(l, g):
            b, free = banks.take()
            for half in range(2):
                wh, wl, tw = W.take(("ada", l, g, half), 4, 512)
                for k in range(4):
                    kk = 4 * half + k
                    lhs = CB[:, 4 * kk:4 * kk + P]
                    mm(b[:, :], lhs, wh[:, k, :], kk == 0, False, tw, t_cb, free)
                    last = mm(b[:, :], lhs, wl[:, k, :], False, kk == 7, signal=(k == 3))
                W.done(last)
            r, rfree = tmps.take()
            tc = copy_a(TMP[0:4, r, :], b[0:4, :], last, rfree)
            banks.give(b, tc)
            pending.append((l, g, r, tc))
            if len(pending) > 1:
                ada_finish()

        def ada_finish():
            l, g, r, tc = pending.pop(0)
            b, free = banks.take()
            for j in range(4):
                last = mm(b[:, 2 * j:2 * j + 2], TMP[0:4, r, P * j:P * j + P], CONST[0:4, CO["sel"]:CO["sel"] + 2],
                          True, True, tc, t_const, free, signal=(j == 3))
            tmps.give(r, last)
            bias = small_at("adab", 48 * l + 4 * g, 4).unsqueeze(2).to_broadcast([P, 4, 2])
            td = tt(dve, ADA[:, l, 4 * g:4 * g + 4, :], b[:, 0:8].rearrange("p (j v) -> p j v", v=2), bias, ALU.add,
                    last, t_small)
            banks.give(b, td)
            t_ada[l, g] = td

        def ada_param(l, p, m, v):
            return ADA[:, l, 8 * p + m, v:v + 1]

        def ada_tokens(l, p):
            return [t_ada[l, 2 * p], t_ada[l, 2 * p + 1]]

        def gain(l, which):
            p = 1 if which == 0 else 4
            g = small_at("nmix" if which == 0 else "nffn", 8 * l, 8).unsqueeze(2).to_broadcast([P, 8, 2])
            return stt(AMOD[:, l, which, :, :], ADA[:, l, 8 * p:8 * p + 8, :], 1.0, g, ALU.add, ALU.mult,
                       ada_tokens(l, p))

        t_ms = [None]
        t_rs = [None]
        t_rsread = [None]

        def rms(T, tx):
            nt = T // P
            b, free = banks.take()
            for m in range(DT):
                i, tfree = tmps.take()
                sq = TMP[:, i, 0:T]
                ta = activ(sq, X[:, m, 0:T], ACT.Square, tx[m], tfree)
                for q in range(nt):
                    last = mm(b[:, q:q + 1], TMP[:, i, q * P:q * P + P], ONE, m == 0 and q == 0, m == DT - 1, ta,
                              t_const, free, signal=(q == nt - 1), loose=True)
                tmps.give(i, last)
            td = ts(MS[:, 0:nt], b[:, 0:nt], 1.0 / D, EPS, ALU.mult, ALU.add, last, t_rs[0])
            banks.give(b, td)
            tp = tt(pool, RS[:, 0:nt], MS[:, 0:nt], const_at("mhalf").to_broadcast([P, nt]), ALU.pow, td, t_rsread[0])
            t_rs[0] = tp
            b, free = banks.take()
            for q in range(nt):
                last = mm(b[:, q * P:q * P + P], RS[:, q:q + 1].to_broadcast([P, P]), IDENT, True, True, tp, free,
                          signal=(q == nt - 1))
            t_rsread[0] = last
            return b, last

        t_nread = [None]

        def norm_split(T, tx, scale, shift, tpar):
            b, tb = rms(T, tx)
            out_t = []
            halves = [(0, 0, 256)] if T == 256 else [(0, 0, 256), (1, 256, 512)]
            for m in range(DT):
                i, tfree = tmps.take()
                got = []
                for v, a, z in halves:
                    x = TMP[:, i, a:z]
                    t1 = stt(x, X[:, m, a:z], scale(m, v), b[:, a:z], ALU.mult, ALU.mult, tb, tpar, tfree)
                    if shift is None:
                        t2 = copy_a(NH[:, m, a:z], x, t1, t_nread[0])
                        t3 = tt(pool, NL[:, m, a:z], x, NH[:, m, a:z].bitcast(F32), ALU.subtract, t2)
                    else:
                        sh = shift(m, v)
                        t2 = activ(NH[:, m, a:z], x, ACT.Identity, t1, t_nread[0], bias=sh)
                        t3 = stt(NL[:, m, a:z], x, sh, NH[:, m, a:z].bitcast(F32), ALU.add, ALU.subtract, t2)
                    got.append(t3)
                tmps.give(i, got)
                out_t.append(got)
            banks.give(b, t1)
            return out_t

        def wide(key, nk, T, xh, xl, tx, t0=0):
            wh, wl, tw = W.take(key, nk, 256)
            outs = []
            if T == 256:
                b, free = banks.take()
                outs = [(b, b[:, 0:256], free), (b, b[:, 256:512], free)]
            else:
                for _ in range(2):
                    b, free = banks.take()
                    outs.append((b, b[:, :], free))
            for j, (b, o, free) in enumerate(outs):
                for k in range(nk):
                    last = mm3(o, wh[:, k, P * j:P * j + P], wl[:, k, P * j:P * j + P], xh[:, k, t0:t0 + T],
                               xl[:, k, t0:t0 + T], k == 0, k == nk - 1, tw, tx[k], free, signal=(k == nk - 1))
                outs[j] = (b, o, last)
            W.done(last)
            return outs

        def tall(key, n, nt, tx):
            wh, wl, tw = W.take(key, 8, 256 if n == 256 else n)
            res = []
            for q in range(nt):
                if q % 2 == 0:
                    b, free = banks.take()
                o = b[:, 256 * (q % 2):256 * (q % 2) + n]
                for k in range(8):
                    c = slice(q * P, q * P + P)
                    last = mm3(o, NH[:, k, c], NL[:, k, c], wh[:, k, 0:n], wl[:, k, 0:n], k == 0, k == 7,
                               tw, tx[k], free, signal=(k == 7))
                if q % 2 == 1:
                    res.append((b, last))
            W.done(last)
            return res

        def rotate(o, src, tsrc, C, S, scale, bank=None):
            n, w = src.shape[1], src.shape[2]
            i, f1 = tmps.take()
            j, f2 = tmps.take()
            a = TMP[:, i, 0:n * w].rearrange("p (n w) -> p n w", n=n)
            s = TMP[:, j, 0:n * w].rearrange("p (n w) -> p n w", n=n)
            Cb, Sb = (q.unsqueeze(1).to_broadcast([P, n, w]) for q in (C, S))
            ta = copy_a(a, src, tsrc, f1, scale=scale)
            hop = w_hop[0]
            tb = shuffle(s, a, hop, ta, f2)
            tc = tt(pool, o, a, Cb, ALU.mult, ta, t_const)
            td = tt(dve, s, s, Sb, ALU.mult, tb, t_const)
            te = tt(dve, o, o, s, ALU.add, tc, td)
            tmps.give(i, [tb, tc])
            tmps.give(j, te)
            return ta, te

        w_hop = [None]

        def split_from(oh, ol, src, scale_ap, scale, tsrc, *w):
            s = scale_ap if scale_ap is not None else scale
            ta = activ(oh, src, ACT.Copy, tsrc, *w, scale=s)
            tb = stt(ol, src, s, oh.bitcast(F32), ALU.mult, ALU.subtract, ta, *w)
            return tb

        def run_jobs(jobs, fillers, every=1):
            jobs, fillers, live, n = deque(jobs), deque(fillers), deque(), 0
            while jobs or live:
                for g in list(live):
                    try:
                        next(g)
                    except StopIteration:
                        live.remove(g)
                if jobs:
                    g = jobs.popleft()
                    next(g)
                    live.append(g)
                n += 1
                if fillers and n % every == 0:
                    fillers.popleft()()
            while fillers:
                fillers.popleft()()

        t_xt = [[t_x[m // 4]] for m in range(DT)]

        def attend_diff(h, qt, Q, K, V, tqk, tv, O, tofree, done):
            k0 = 0 if qt < 2 else 256
            nk = 512 - k0
            st, sfree = stats.take()
            nm, sm, r, ratio = (STAT[:, st, 2 * i:2 * i + 2] for i in range(4))
            pt = []
            for j in range(2):
                b, free = banks.take()
                ps = slice(64 * j, 64 * j + 64)
                tm = mm(b[:, 0:nk], Q[ps, h, qt * P:qt * P + P], K[ps, h, k0:512], True, True, tqk, free, signal=True)
                t1 = reduce(nm[:, j:j + 1], b[:, 0:nk], ALU.max, True, tm, sfree)
                i, tfree = tmps.take()
                t2 = activ(TMP[:, i, 0:nk], b[:, 0:nk], ACT.Exp, t1, tfree, bias=nm[:, j:j + 1], accum_out=sm[:, j:j + 1])
                banks.give(b, t2)
                pt.append((i, t2))
            t3 = recip(r, sm, pt[0][1], pt[1][1], sfree)
            t4 = stt(ratio[:, 0:1], sm[:, 0:1], r[:, 1:2], LAMV[:, 0:1], ALU.mult, ALU.mult, t3, t_lam)
            (i0, ta), (i1, tb) = pt
            t5 = stt(TMP[:, i0, 0:nk], TMP[:, i1, 0:nk], ratio[:, 0:1], TMP[:, i0, 0:nk], ALU.mult, ALU.add, t4, ta, tb)
            tmps.give(i1, t5)
            yield
            yield
            b, free = banks.take()
            for k in range(nk // P):
                tm = tr(b[:, k * P:k * P + P], TMP[:, i0, k * P:k * P + P], t5, free, signal=(k == nk // P - 1))
            tmps.give(i0, tm)
            i, tfree = tmps.take()
            te = copy_a(TMP[:, i, 0:nk], b[:, 0:nk], tm, tfree)
            banks.give(b, te)
            yield
            b, free = banks.take()
            for k in range(nk // P):
                tm = mm(b[:, 0:P], TMP[:, i, k * P:k * P + P], V[:, k0 // P + k, h * P:h * P + P], k == 0,
                        k == nk // P - 1, te, tv, free, signal=(k == nk // P - 1))
            tmps.give(i, tm)
            ss, ms, rs, f = (STAT[:, st, 8 + i:9 + i] for i in range(4))
            j, jfree = tmps.take()
            t6 = activ(TMP[:, j, 0:P], b[:, 0:P], ACT.Square, tm, t3, jfree, sfree, scale=r[:, 0:1], accum_out=ss)
            tmps.give(j, t6)
            t7 = ts(ms, ss, 1.0 / P, EPS, ALU.mult, ALU.add, t6, sfree)
            t8 = tt(pool, rs, ms, const_at("mhalf"), ALU.pow, t7, sfree, t_const)
            yield
            t9 = tt(dve, f, rs, r[:, 0:1], ALU.mult, t8)
            t10 = ts(TMP[:, O, qt * P:qt * P + P], b[:, 0:P], f, None, ALU.mult, None, t9, tofree)
            banks.give(b, t10)
            stats.give(st, t10)
            done.append(t10)
            yield
            if qt == 3:
                yield
                b, free = banks.take()
                for q in range(4):
                    tm = tr(b[:, q * P:q * P + P], TMP[:, O, q * P:q * P + P], done, free, signal=(q == 3))
                tmps.give(O, tm)
                tl = split_from(NH[:, h, :], NL[:, h, :], b[:, :], LAMV[:, 1:2], None, tm, t_lam, t_nread[0])
                banks.give(b, tl)
                t_o[h] = tl

        t_o = {}

        def attend_na(h, qt, Q, K, V, tqk, tv, bias, tbias, O, tofree, done, bias_done):
            m, e2 = h // 2, h % 2
            st, sfree = stats.take()
            nm, sm, r = (STAT[:, st, i:i + 1] for i in range(3))
            b, free = banks.take()
            ps = slice(64 * e2, 64 * e2 + 64)
            tm = mm(b[:, :], Q[ps, m, qt * P:qt * P + P], K[ps, m, :], True, True, tqk, free, signal=True)
            t0 = tt(dve, b[:, 0:256], b[:, 0:256], bias, ALU.add, tm, tbias)
            bias_done.append(t0)
            t1 = reduce(nm, b[:, :], ALU.max, True, t0, sfree)
            i0, tfree = tmps.take()
            t2 = activ(TMP[:, i0, :], b[:, :], ACT.Exp, t1, tfree, bias=nm, accum_out=sm)
            banks.give(b, t2)
            t3 = recip(r, sm, t2, sfree)
            yield
            yield
            b, free = banks.take()
            for k in range(4):
                tm = tr(b[:, k * P:k * P + P], TMP[:, i0, k * P:k * P + P], t2, free, signal=(k == 3))
            tmps.give(i0, tm)
            i, tfree = tmps.take()
            te = copy_a(TMP[:, i, :], b[:, :], tm, tfree)
            banks.give(b, te)
            yield
            b, free = banks.take()
            for k in range(4):
                tm = mm(b[:, 0:64], TMP[:, i, k * P:k * P + P], V[:, k, h * 64:h * 64 + 64], k == 0, k == 3, te, tv,
                        free, signal=(k == 3))
            tmps.give(i, tm)
            c = qt * P + e2 * 64
            t4 = ts(TMP[:, O, c:c + 64], b[:, 0:64], r, None, ALU.mult, None, tm, t3, tofree)
            banks.give(b, t4)
            stats.give(st, t4)
            done.append(t4)
            yield
            if len(done) == 4:
                b, free = banks.take()
                for q in range(2):
                    tm = tr(b[:, q * P:q * P + P], TMP[:, O, q * P:q * P + P], done, free, signal=(q == 1))
                tmps.give(O, tm)
                tl = split_from(NH[:, m, 0:256], NL[:, m, 0:256], b[:, 0:256], None, 1.0, tm, t_nread[0])
                banks.give(b, tl)
                t_o[m] = tl

        def residual(outs, m0, T, gate, tg):
            for j, (b, o, tm) in enumerate(outs):
                m = m0 + j
                for v in range(T // 256):
                    c = slice(256 * v, 256 * v + 256)
                    t = stt(X[:, m, c], o[:, c], gate(m, v), X[:, m, c], ALU.mult, ALU.add, tm, tg, t_xt[m], t_xr)
                t_xt[m] = [t]
            for b in {id(o[0]): o[0] for o in outs}.values():
                banks.give(b, t)

        t_xr = []
        fill = deque()

        def fillers(n):
            for _ in range(n):
                if fill:
                    fill.popleft()()

        def ffn(l, T, tn):
            stack = ExitStack()
            nch = 2 if T == 512 else 1
            nj = FT // nch
            HH = sb(f"HH{l}", [P, nj, T], F32R, stack)
            HL = sb(f"HL{l}", [P, nj, T], F32R, stack)
            ns = T // 256
            t_hread = None
            for c in range(nch):
                th = []
                for jj in range(nj):
                    j = c * nj + jj
                    outs = wide(("up", l, j), 8, T, NH, NL, tn)
                    acc = []
                    for s, (b, o, tm) in enumerate(outs):
                        col = 44 * l + j + FT * s
                        w = lambda tap, j=j, s=s: small_at("fconv", (3 * l + tap) * 44 + j + FT * s)
                        i, tfree = tmps.take()
                        a = TMP[:, i, 0:T]
                        a3 = a.rearrange("p (n w) -> p n w", n=ns)
                        o3 = o.rearrange("p (n w) -> p n w", n=ns)
                        if T == 256:
                            tm = outs[1][2]
                        t1 = activ(a, o, ACT.Identity, tm, tfree, scale=w(1), bias=small_at("fconvb", col))
                        acc.append([i, a, a3, o3, t1, w, b])
                    for s in range(2):
                        i, a, a3, o3, t1, w, b = acc[s]
                        first = [acc[0][4], acc[1][4]] if T == 256 else t1
                        t2 = stt(a3[:, :, 1:256], o3[:, :, 0:255], w(0), a3[:, :, 1:256], ALU.mult, ALU.add, first)
                        t3 = stt(a3[:, :, 0:255], o3[:, :, 1:256], w(2), a3[:, :, 0:255], ALU.mult, ALU.add, t2)
                        acc[s][4] = t3
                        if T != 256:
                            banks.give(b, t3)
                    if T == 256:
                        banks.give(b, t3)
                    (ia, aa, _, _, ta, _, _), (ig, ag, _, _, tg, _, _) = acc
                    t4 = activ(ag, ag, ACT.Silu, tg)
                    t5 = tt(dve, aa, aa, ag, ALU.mult, t4, ta)
                    tmps.give(ig, t5)
                    t6 = copy_a(HH[:, jj, :], aa, t5, t_hread)
                    t7 = tt(pool, HL[:, jj, :], aa, HH[:, jj, :].bitcast(F32), ALU.subtract, t6)
                    tmps.give(ia, t7)
                    th.append([t6, t7])
                t_nread[0] = outs[1][2]
                for m in range(DT):
                    b, free = banks.take()
                    for half in range(nj // HALF_FT):
                        wh, wl, tw = W.take(("down", l, c if nch == 2 else half, m), HALF_FT, 128)
                        for k in range(HALF_FT):
                            kk = half * HALF_FT + k
                            last = mm3(b[:, 0:T], wh[:, k, :], wl[:, k, :], HH[:, kk, :], HL[:, kk, :], kk == 0,
                                       kk == nj - 1, tw, th[kk], free, signal=(k == HALF_FT - 1))
                        W.done(last)
                    residual([(b, b[:, 0:T], last)], m, T, lambda m, v: ada_param(l, 5, m, v), ada_tokens(l, 5))
                t_hread = last
            stack.close()
            return t_hread

        lamv = lambda a, n: SMALL[:, SM["lam"] + a:SM["lam"] + a + n]
        tl1 = tt(dve, LAMV[:, 4:5].to_broadcast([P, 1]), small_at("subln", 0), ONE, ALU.bypass, t_small, t_const)
        i, tfree = tmps.take()
        tl = []
        for j in range(2):
            t = tt(dve, TMP[:, i, 64 * j:64 * j + 64], lamv(128 * j, 64), lamv(128 * j + 64, 64), ALU.mult, t_small)
            tl.append(reduce(LAMV[:, 2 + j:3 + j], TMP[:, i, 64 * j:64 * j + 64], ALU.add, False, t))
        tmps.give(i, tl)
        t = activ(LAMV[:, 4:6], LAMV[:, 2:4], ACT.Exp, tl, tl1)
        t = tt(dve, LAMV[:, 6:7], LAMV[:, 5:6], LAMV[:, 4:5], ALU.subtract, t)
        t1 = ts(LAMV[:, 0:1], LAMV[:, 6:7], -LAM_INIT, None, ALU.add, None, t)
        t2 = ts(LAMV[:, 1:2], small_at("subln", 0), 1.0 - LAM_INIT, None, ALU.mult, None, t_small)
        t_lam = [t1, t2]

        for g in range(4):
            ada_group(0, g)
        ada_finish()

        for l in range(2):
            Tq = 512 if l == 0 else 256
            tg = gain(l, 0)
            t_am = [tg, ada_tokens(l, 0)]
            tn = norm_split(512, t_xt, lambda m, v: AMOD[:, l, 0, m, v:v + 1], lambda m, v: ada_param(l, 0, m, v), t_am)
            stack = ExitStack()
            new_scope()
            Q = sb(f"Q{l}", [P, DT, Tq], F32, stack)
            K = sb(f"K{l}", [P, DT, 512], F32, stack)
            V = sb(f"V{l}", [P, 4, D], F32, stack)
            hop = [16 + i for i in range(16)] + list(range(16))
            w_hop[0] = hop
            tqk = {}
            rest = [lambda g=g: ada_group(0, g) for g in range(4, 12)] if l == 0 else []
            for i in range(8):
                isq = i < 4
                T = Tq if isq else 512
                outs = wide(("qkv", l, i), 8, T, NH, NL, tn)
                dst = Q if isq else K
                scale = 0.125 if isq else 1.0
                if T == 256:
                    m = 2 * i
                    t = copy_a(dst[:, m:m + 2, :], outs[0][0][:, :].rearrange("p (n w) -> p n w", n=2), outs[1][2],
                               scale=scale)
                    banks.give(outs[0][0], t)
                    tqk["q", m] = tqk["q", m + 1] = [t]
                else:
                    for j, (b, o, tm) in enumerate(outs):
                        m = 2 * (i % 4) + j
                        if l == 0:
                            tc = copy_a(dst[:, m, 256:512], o[:, 256:512], tm, scale=scale)
                            ta, te = rotate(dst[:, m:m + 1, 0:256], o[:, 0:256].unsqueeze(1), tm,
                                            const_at("c1", 0, 256), const_at("s1", 0, 256), scale)
                            banks.give(b, [tc, ta])
                            tqk["q" if isq else "k", m] = [tc, te]
                        else:
                            tc = copy_a(dst[:, m, :], o, tm, scale=scale)
                            banks.give(b, tc)
                            tqk["k", m] = [tc]
                if rest:
                    rest.pop(0)()
            if l == 0:
                ada_finish()
            tv = []
            for i in range(4):
                for q, (b, tm) in enumerate(tall(("qkv", l, 8 + i), 256, 4, tn)):
                    t = copy_a(V[:, 2 * q:2 * q + 2, 256 * i:256 * i + 256],
                               b[:, :].rearrange("p (n w) -> p n w", n=2), tm)
                    banks.give(b, t)
                tv.append(t)
                t_nread[0] = tm
            if l == 0:
                jobs = []
                fl = [lambda g=g: ada_group(1, g) for g in range(12)] + [ada_finish]
                for h in range(DT):
                    holder = {}

                    def job(h, qt, holder):
                        if qt == 0:
                            holder["O"], holder["free"] = tmps.take()
                            holder["done"] = []
                        yield from attend_diff(h, qt, Q, K, V, [tqk["q", h], tqk["k", h]], tv, holder["O"],
                                               holder["free"], holder["done"])

                    jobs += [job(h, qt, holder) for qt in range(4)]
                run_jobs(jobs, fl, every=2)
            else:
                BI = sb("BI", [P, 2, 2, 16, 64], F32, stack)
                BR = sb("BR", [P, 2, 16, 64], F32, stack)
                t_bfree = {0: [], 1: []}
                t_b = {}
                t_rev = [None]

                def load_bias(ch):
                    s = ch % 2
                    for r in range(4):
                        base = 64 + ((r * 16 + 4 * ch) * 4) * 31 + 15 - 63
                        src = bass.AP(rpb.tensor, base, [[1, 64], [31, 16], [1, 64]])
                        p0 = 64 * (r % 2)
                        t = act.dma(lambda e, s=s, r=r, src=src, p0=p0: e.dma_start(
                            BR[p0:p0 + 64, r // 2, :, :], src), d_bias[s], t_rev[0])
                    rev = bass.AP(BR[:, :, :, :].tensor, 63, [[2048, P], [64, 32], [-1, 64]])
                    v = BI[:, s, :, :, :].rearrange("p a r c -> p (a r) c")
                    t_b[ch] = tt(pool, v, rev, const_at("mna", 0, 64).unsqueeze(1).to_broadcast([P, 32, 64]), ALU.add,
                                 t, t_bfree[s])
                    t_rev[0] = t_b[ch]

                load_bias(0)
                load_bias(1)
                bias_done = {c: [] for c in range(4)}
                jobs = []

                def job(m, qt, e2, holder):
                    if "O" not in holder:
                        holder["O"], holder["free"] = tmps.take()
                        holder["done"] = []
                    h = 2 * m + e2
                    ch = h // 4
                    if h % 4 == 0 and qt == 0 and ch in (1, 2):
                        t_bfree[(ch + 1) % 2] = list(bias_done[ch - 1])
                        load_bias(ch + 1)
                    bias = BI[:, ch % 2, qt, 4 * (h % 4):4 * (h % 4) + 4, :]
                    yield from attend_na(h, qt, Q, K, V, [tqk["q", m], tqk["k", m]], tv,
                                         bias.rearrange("p r c -> p (r c)"), t_b[ch], holder["O"], holder["free"],
                                         holder["done"], bias_done[ch])

                for m in range(DT):
                    holder = {}
                    jobs += [job(m, qt, e2, holder) for qt in range(2) for e2 in range(2)]
                run_jobs(jobs, [])
            stack.close()
            to = [[t_o[m]] for m in range(DT)]
            for i in range(4):
                outs = wide(("wo", l, i), 8, Tq, NH, NL, to)
                if Tq == 256:
                    outs[0] = (outs[0][0], outs[0][1], outs[1][2])
                residual(outs, 2 * i, Tq, lambda m, v: ada_param(l, 2, m, v), ada_tokens(l, 2))
            t_nread[0] = outs[1][2]
            tg = gain(l, 1)
            t_am = [tg, ada_tokens(l, 3)]
            tn = norm_split(Tq, t_xt, lambda m, v: AMOD[:, l, 1, m, v:v + 1], lambda m, v: ada_param(l, 3, m, v), t_am)
            ffn(l, Tq, tn)

        def gain_in_place(name):
            b, tb = rms(256, t_xt)
            for m in range(DT):
                t = stt(X[:, m, 0:256], X[:, m, 0:256], small_at(name, m), b[:, 0:256], ALU.mult, ALU.mult, tb, t_xt[m])
                t_xt[m] = [t]
            banks.give(b, t)

        gain_in_place("nout")

        new_scope()
        late_sb[0] = sb("LATEC", [P, NLATE])
        t_late = act.dma(lambda e: e.dma_start(late_sb[0][:, :], late), d_late)
        for q in (dve, pool, act, pe):
            q.wait_for([t_late])
        for l in range(2):
            tn = norm_split(256, t_xt, lambda m, v: small_at("normg", 8 * l + m), None, t_small)
            stack = ExitStack()
            new_scope()
            mk = lambda name, shape, dt=F32: sb(f"{name}_{l}", shape, dt, stack)
            QN, KN = mk("QN", [P, 2, 256]), mk("KN", [P, 2, 256])
            KC = mk("KC", [P, 2, 256])
            VN = mk("VN", [P, 2, 144])
            VF = mk("VF", [P, 2, 256])
            QF, KF = mk("QF", [P, 2, 256]), mk("KF", [P, 2, 256])
            PU = mk("PU", [P, 2, 2, 272])
            CXY = mk("CXY", [P, 2, 258])
            CBG = mk("CBG", [P, 2, 256])
            G = mk("G", [P, 8, 256])
            M = mk("M", [P, 2, 8, 256])
            LF = mk("LF", [P, 2, 128])
            CR = mk("CR", [P, 256])
            NCR = mk("NCR", [P, 256])
            ON = mk("ON", [P, 2, 256])
            OF = mk("OF", [P, 2, 256])
            ZH, ZL = (t[:, :, 256:512].rearrange("p (n k) w -> p n k w", n=4) for t in (NH, NL))
            ACC = X[:, :, 256:512]
            iflt, t_flt = tmps.take()
            FLT = TMP[:, iflt, :].rearrange("p (n w) -> p n w", n=2)
            FH, FL = mk("FH", [P, 2, 256], F32R), mk("FL", [P, 2, 256], F32R)
            CM = mk("CM", [P, 640])
            w_hop[0] = [8 + i for i in range(8)] + list(range(8)) + list(range(16, 32))
            pair = lambda b: b[:, :].rearrange("p (n w) -> p n w", n=2)
            tk = {}

            def proj(i):
                outs = wide(("in", l, i), 8, 256, NH, NL, tn)
                t_nread[0] = outs[1][2]
                return outs[0][0], outs[1][2]

            def plain(i, dst, name, scale=1.0):
                b, tm = proj(i)
                t = copy_a(dst, pair(b), tm, scale=scale)
                banks.give(b, t)
                tk[name] = t

            def turned(i, dst, name, scale):
                b, tm = proj(i)
                ta, te = rotate(dst, pair(b), tm, const_at("c2", 0, 256), const_at("s2", 0, 256), scale)
                banks.give(b, ta)
                tk[name] = te

            turned(0, QN[:, :, :], "qn", 0.125)
            turned(1, KN[:, :, :], "kn", 1.0)
            (b, tm), = tall(("in", l, 3), 144, 2, tn)
            t = copy_a(VN[:, :, :], pair(b)[:, :, 0:144], tm)
            banks.give(b, t)
            tk["vn"] = t
            i, tfree = tmps.take()
            z, az, ez, lz, mz = (TMP[:, i, 8 * a:8 * a + 8].rearrange("p (q h) -> p q h", q=2) for a in range(5))
            fb = small_at("foxb", 4 * l, 4).unsqueeze(1).to_broadcast([P, 2, 4])
            t1 = tt(dve, z, VN[:, :, 140:144], fb, ALU.add, tk["vn"], tfree, t_small)
            t2 = activ(az, z, ACT.Abs, t1)
            t3 = activ(ez, az, ACT.Exp, t2, scale=-1.0)
            t4 = activ(lz, ez, ACT.Ln, t3, bias=1.0)
            t5 = ts(mz, z, 0.0, None, ALU.min, None, t1)
            t0 = zero(LF[:, :, :])
            lfv = LF[:, :, :].rearrange("p q (h s) -> p q h s", h=4)[:, :, :, 0]
            t6 = tt(dve, lfv, mz, lz, ALU.subtract, t4, t5, t0)
            tmps.give(i, t6)
            GS = CM[:, 512:536].rearrange("p (q g) -> p q g", q=2)
            t = activ(GS, VN[:, :, 128:140], ACT.Tanh, tk["vn"], scale=0.5)
            tk["gs"] = ts(GS, GS, 0.5, 0.5, ALU.mult, ALU.add, t)
            plain(5, QF[:, :, :], "qf", 0.125)
            plain(6, KF[:, :, :], "kf")
            b, free = banks.take()
            for q in range(2):
                tm = tr(b[:, q * P:q * P + P], LF[:, q, :], t6, free, signal=(q == 1))
            t = scan_sum(CR[:, :], const_at("ones", 0, 256), b[:, 0:256], tm)
            banks.give(b, t)
            tk["cr"] = [t, ts(NCR[:, :], CR[:, :], -1.0, None, ALU.mult, None, t)]
            (b, tm), = tall(("in", l, 4), 256, 2, tn)
            t = copy_a(VF[:, :, :], pair(b), tm)
            banks.give(b, t)
            tk["vf"] = t
            b, tm = proj(2)
            t = copy_a(KC[:, :, :], pair(b), tm)
            banks.give(b, t)
            tk["kc"] = t

            t_f = []
            tz = zero(FLT, t_flt)
            for kind in range(2):
                for par in range(2):
                    ps = slice(64 * par, 64 * par + 64)
                    src = bass.AP(KC[:, :, :].tensor, 64 * par * 512 + kind * 256 + par, [[512, 64], [2, 16], [16, 15]])
                    pos = SMALL[ps, SM["cpos"] + (2 * l + kind) * 16:SM["cpos"] + (2 * l + kind) * 16 + 16]
                    dst = FLT[ps, kind, :].rearrange("p (a n) -> p a n", a=16)[:, :, 0:15]
                    t_f.append(tt(dve, dst, src, pos.unsqueeze(2).to_broadcast([64, 16, 15]), ALU.add, tk["kc"], tz))
            t1 = copy_a(FH[:, :, :], FLT, t_f)
            t_f = tt(dve, FL[:, :, :], FLT, FH[:, :, :].bitcast(F32), ALU.subtract, t1)
            tmps.give(iflt, t_f)
            KCT = CM[:, 0:16]
            VCB = CM[:, 128:384]
            tz = zero(CM[:, 0:384])
            hid = []
            for kind in range(2):
                wh, wl, tw = W.take(("cmp", l, kind), 16, 128)
                b, free = banks.take()
                for k in range(16):
                    last = mm3(b[:, 0:16], wh[:, k, :], wl[:, k, :], FH[:, kind, 16 * k:16 * k + 16],
                               FL[:, kind, 16 * k:16 * k + 16], k == 0, k == 15, tw, t_f, free, signal=(k == 15))
                W.done(last)
                x, th, h2 = (CM[:, 544 + 16 * a + 48 * kind:560 + 16 * a + 48 * kind] for a in range(3))
                t1 = ts(x, b[:, 0:16], small_at("cb1", 2 * l + kind), None, ALU.add, None, last)
                banks.give(b, t1)
                t2 = activ(th, x, ACT.Tanh, t1, scale=0.5)
                t3 = stt(h2, th, 1.0, x, ALU.add, ALU.mult, t2)
                hid.append((h2, t3))
            w2k = small_at("w2", (2 * l) * 128, 128)
            w2v = small_at("w2", (2 * l + 1) * 128, 64)
            b, free = banks.take()
            tm = mm(b[:, 0:16], w2k, hid[0][0], True, True, hid[0][1], free, signal=True)
            i, tfree = tmps.take()
            kc, ks = TMP[:, i, 0:16], TMP[:, i, 16:32]
            t1 = ts(kc, b[:, 0:16], 0.5, small_at("cb2", l), ALU.mult, ALU.add, tm, tfree)
            banks.give(b, t1)
            t2 = shuffle(ks, kc, w_hop[0], t1)
            t3 = tt(dve, KCT, kc, const_at("cmpc", 0, 16), ALU.mult, t1, tz)
            t4 = tt(dve, ks, ks, const_at("cmps", 0, 16), ALU.mult, t2)
            t5 = tt(dve, KCT, KCT, ks, ALU.add, t3, t4)
            tmps.give(i, t5)
            tk["kct"] = t5
            i, tfree = tmps.take()
            hw = TMP[:, i, 0:128].rearrange("p (h n) -> p h n", h=4)
            tz2 = zero(TMP[:, i, 0:128], tfree)
            t1 = copy_v(hw[:, :, 0:15], hid[1][0][:, 0:15].unsqueeze(1).to_broadcast([P, 4, 15]), hid[1][1], tz2)
            b, free = banks.take()
            tm = mm(b[:, 0:64], TMP[:, i, 0:128], w2v, True, True, t1, free, signal=True)
            tmps.give(i, tm)
            tv4 = []
            for h in range(4):
                ps = slice(32 * h, 32 * h + 15)
                b2 = late_sb[0][ps, LATE["cb2v"] + 64 * l:LATE["cb2v"] + 64 * l + 64]
                tv4.append(stt(VCB[ps, 64 * h:64 * h + 64], b[ps, 0:64], 0.5, b2, ALU.mult, ALU.add, tm, tz))
            banks.give(b, tv4[-1])
            tk["vcb"] = tv4

            oparts = {}
            ogive = {}

            def attend_cmp(qt):
                st, sfree = stats.take()
                nm, sm, r = (STAT[:, st, 4 * a:4 * a + 4] for a in range(3))
                b, free = banks.take()
                s3 = b[:, 0:64].rearrange("p (h n) -> p h n", h=4)[:, :, 0:15]
                tm = None
                for h in (0, 2, 1, 3):
                    ps = slice(64 * (h % 2), 64 * (h % 2) + 64)
                    tm = mm(b[:, 16 * h:16 * h + 15], QN[ps, h // 2, qt * P:qt * P + P], KCT[ps, 0:15], True, True,
                            tk["qn"], tk["kct"], free, tm, signal=(h > 1))
                i, tfree = tmps.take()
                e3 = TMP[:, i, 0:128].rearrange("p (h n) -> p h n", h=4)
                tz = zero(TMP[:, i, 0:128], tfree)
                e15 = e3[:, :, 0:15]
                over = lambda name: const_at(name, 16 * qt, 15).unsqueeze(1).to_broadcast([P, 4, 15])
                t1 = tt(dve, s3, s3, over("cmpadd"), ALU.add, tm)
                t2 = reduce(nm, s3, ALU.max, True, t1, sfree)
                t3 = tt(dve, e15, s3, nm.unsqueeze(2).to_broadcast([P, 4, 15]), ALU.add, t2, tz)
                banks.give(b, t3)
                t4 = activ(e15, e15, ACT.Exp, t3)
                t5 = reduce(sm, e15, ALU.add, False, t4)
                t6 = recip(r, sm, t5)
                t7 = tt(dve, e15, e15, over("cmpmul"), ALU.mult, t5)
                t8 = tt(dve, e15, e15, r.unsqueeze(2).to_broadcast([P, 4, 15]), ALU.mult, t6, t7)
                stats.give(st, t8)
                yield
                yield
                b, free = banks.take()
                tm = tr(b[:, 0:P], TMP[:, i, 0:P], t8, free, signal=True)
                tmps.give(i, tm)
                j, jfree = tmps.take()
                te = copy_a(TMP[:, j, 0:P], b[:, 0:P], tm, jfree)
                banks.give(b, te)
                yield
                b, free = banks.take()
                tm = mm(b[:, 0:256], TMP[:, j, 0:P], VCB, True, True, te, tk["vcb"], free, signal=True)
                tmps.give(j, tm)
                g = GS[:, qt, 0:4].unsqueeze(2).to_broadcast([P, 4, 64])
                o = ON[:, qt, :].rearrange("p (h d) -> p h d", h=4)
                t = tt(dve, o, b[:, 0:256].rearrange("p (h d) -> p h d", h=4), g, ALU.mult, tm, tk["gs"])
                banks.give(b, t)
                oparts["nsa", qt] = t

            def attend_causal(kind, qt):
                nk = P * (qt + 1)
                per = 512 // nk
                order_h = (0, 2, 1, 3)
                fox = kind == 2
                st, sfree = stats.take()
                nm, sm, r = (STAT[:, st, 4 * a:4 * a + 4] for a in range(3))
                nmr = nm.rearrange("p (l r) -> p r l", r=2)
                ptiles = []
                for g in range(4 // per):
                    b, free = banks.take()
                    tm = None
                    for a in range(per):
                        h = order_h[g * per + a]
                        ps = slice(64 * (h % 2), 64 * (h % 2) + 64)
                        o = b[:, a * nk:a * nk + nk]
                        if fox:
                            q, k, tqk = QF[ps, h // 2, qt * P:qt * P + P], KF[ps, h // 2, 0:nk], [tk["qf"], tk["kf"]]
                        else:
                            q, k, tqk = QN[ps, h // 2, qt * P:qt * P + P], KN[ps, kind, 0:nk], [tk["qn"], tk["kn"]]
                        tm = mm(o, q, k, True, not fox, tqk, free, tm if a == 2 or fox else None, signal=True)
                        if fox:
                            rw = slice(32 * h, 32 * h + 1)
                            ones = CONST[rw, CO["ones"]:CO["ones"] + 256]
                            mm(o, CR[rw, qt * P:qt * P + P], ones[:, 0:nk], False, False, tk["cr"], tm)
                            tm = mm(o, ones[:, 0:P], NCR[rw, 0:nk], False, True, signal=True)
                    b3 = b[:, :].rearrange("p (a k) -> p a k", a=per)
                    dg = b3[:, :, nk - P:nk]
                    t1 = tt(dve, dg, dg, const_at("causal", 0, P).unsqueeze(1).to_broadcast([P, per, P]), ALU.add, tm)
                    if per == 4:
                        t2 = reduce(nmr, b[:, :].rearrange("p (r l k) -> p r l k", r=2, l=2), ALU.max, True, t1, sfree)
                    else:
                        t2 = reduce(nmr[:, g, :], b3, ALU.max, True, t1, sfree)
                    i, tfree = tmps.take()
                    for a in range(per):
                        h = order_h[g * per + a]
                        t3 = activ(TMP[:, i, a * nk:a * nk + nk], b[:, a * nk:a * nk + nk], ACT.Exp, t2, tfree,
                                   bias=nm[:, h:h + 1], accum_out=sm[:, h:h + 1])
                    banks.give(b, t3)
                    ptiles.append((i, t3))
                t4 = recip(r, sm, ptiles[-1][1], sfree)
                if kind < 2:
                    t4 = tt(dve, r, r, GS[:, qt, 4 + 4 * kind:8 + 4 * kind], ALU.mult, t4, tk["gs"])
                yield
                yield
                turned_ = []
                for i, t3 in ptiles:
                    b, free = banks.take()
                    for a in range(4):
                        tm = tr(b[:, a * P:a * P + P], TMP[:, i, a * P:a * P + P], t3, free, signal=(a == 3))
                    tmps.give(i, tm)
                    j, jfree = tmps.take()
                    te = copy_a(TMP[:, j, :], b[:, :], tm, jfree)
                    banks.give(b, te)
                    turned_.append((j, te))
                yield
                b, free = banks.take()
                for n, h in enumerate(order_h):
                    j, te = turned_[n // per]
                    for k in range(qt + 1):
                        c = ((n % per) * (qt + 1) + k) * P
                        v = VF[:, k, 64 * h:64 * h + 64] if kind == 2 else VN[:, k, 64 * kind:64 * kind + 64]
                        tm = mm(b[:, 64 * h:64 * h + 64], TMP[:, j, c:c + P], v, k == 0, k == qt, te,
                                tk["vf"] if kind == 2 else tk["vn"], free, signal=(k == qt and n % per == per - 1))
                    if n % per == per - 1:
                        tmps.give(j, tm)
                o = (OF if kind == 2 else ON)[:, qt, :].rearrange("p (h d) -> p h d", h=4)
                r3 = r.unsqueeze(2).to_broadcast([P, 4, 64])
                v3 = b[:, 0:256].rearrange("p (h d) -> p h d", h=4)
                if kind == 2:
                    t = tt(dve, o, v3, r3, ALU.mult, tm, t4)
                    banks.give(b, t)
                    oparts["fox", qt] = t
                else:
                    i, tfree = tmps.take()
                    x3 = TMP[:, i, 0:256].rearrange("p (h d) -> p h d", h=4)
                    t = tt(dve, x3, v3, r3, ALU.mult, tm, t4, tfree)
                    banks.give(b, t)
                    t = tt(dve, o, o, x3, ALU.add, t, oparts["nsa", qt])
                    tmps.give(i, t)
                    oparts["nsa", qt] = t
                stats.give(st, t)

            def gates(i):
                b, tm = proj(11 + i)
                j, tfree = tmps.take()
                t = activ(TMP[:, j, :], b[:, :], ACT.Tanh, tm, tfree, scale=0.5)
                g = G[:, 2 * i:2 * i + 2, :]
                t = stt(g, TMP[:, j, :].rearrange("p (n w) -> p n w", n=2), 1.0, pair(b), ALU.add, ALU.mult, t)
                banks.give(b, t)
                tmps.give(j, t)
                tk["g", i] = t

            order = (1, 2, 0, 3)
            m_free = [[], []]

            def merge(n_, j):
                b, tm = proj(15 + 4 * order[n_] + j)
                dst = M[:, n_ % 2, 2 * j:2 * j + 2, :]
                t = activ(dst, pair(b), ACT.Tanh, tm, m_free[n_ % 2], scale=0.5)
                banks.give(b, t)
                tk["m", order[n_], j] = t

            def gated(n, src, tsrc):
                i, tfree = tmps.take()
                zf = TMP[:, i, :].rearrange("p (n w) -> p n w", n=2)
                t1 = tt(dve, zf, src, G[:, 2 * n:2 * n + 2, :], ALU.mult, tsrc, tk["g", n], tfree)
                t2 = split_from(ZH[:, n, :, :], ZL[:, n, :, :], zf, None, 0.5, t1)
                tmps.give(i, t2)
                tk["z", n] = t2
                return t1

            def pooling():
                b, tm = proj(7)
                tz = zero_p(PU[:, :, :, 0:16])
                u0 = PU[:, 0, :, 16:272]
                t = copy_a(u0, pair(b), tm)
                banks.give(b, t)
                tz2 = [tz, t]
                cur = 0
                t_p = tz2

                def rows_of(s, c, sh, lo=0, hi=P):
                    return PU[lo:hi, s, c, 16 - sh:272 - sh]

                a = PU[:, 1, :, 16:272]
                t1 = tt(dve, a, PU[:, 0, :, 16:272], PU[:, 0, :, 15:271], ALU.add, t_p)
                i, f1 = tmps.take()
                S4 = TMP[:, i, :]
                ps = slice(64, 128)
                t4a = tt(dve, S4[ps, 0:256], PU[ps, 1, 0, 16:272], PU[ps, 1, 0, 14:270], ALU.add, t1, f1)
                w4 = PW[:, 0, :]
                w8 = PW[:, 1, :]
                t4b = tt(dve, w4[:, 16:272], PU[:, 1, 1, 16:272], PU[:, 1, 1, 14:270], ALU.add, t1, t_pw)
                t8 = tt(dve, w8[:, 16:272], w4[:, 16:272], w4[:, 12:268], ALU.add, t4b)
                t16 = tt(dve, S4[ps, 256:512], w8[ps, 16:272], w8[ps, 8:264], ALU.add, t8, f1)
                lo = slice(0, 64)
                tc1 = copy_v(S4[lo, 0:256], PU[lo, 1, 0, 16:272], t1, f1)
                tc2 = copy_v(S4[lo, 256:512], w8[lo, 16:272], t8, f1)
                t = tt(dve, S4, S4, const_at("icnt", 0, 512), ALU.mult, t4a, t16, tc1, tc2)
                s3 = S4.rearrange("p (n w) -> p n w", n=2)
                t = tt(dve, s3, s3, PU[:, 0, :, 16:272], ALU.subtract, t)
                b, free = banks.take()
                for c in range(2):
                    w = small_at("poolw", (2 * l + c) * 128, 128)
                    tm = mm(b[:, 256 * c:256 * c + 256], w, S4[:, 256 * c:256 * c + 256], True, True, t, free,
                            signal=(c == 1))
                i2, f2 = tmps.take()
                for c in range(2):
                    t = ts(TMP[:, i2, 256 * c:256 * c + 256], b[:, 256 * c:256 * c + 256],
                           small_at("pscale", 2 * l + c), None, ALU.mult, None, tm, f2)
                banks.give(b, t)
                tmps.give(i, tm)
                tg = gated(1, TMP[:, i2, :].rearrange("p (n w) -> p n w", n=2), t)
                tmps.give(i2, tg)

            PW = mk("PW", [P, 2, 272])
            t_pw = zero_p(PW[:, :, 0:16])


            def conv_in():
                b, tm = proj(8)
                i, tfree = tmps.take()
                t = copy_a(TMP[:, i, :], b[:, :], tm, tfree)
                banks.give(b, t)
                b, tm = proj(9)
                t2 = copy_a(CBG[:, :, :], pair(b), tm)
                banks.give(b, t2)
                tk["cbg"] = t2
                b, tm = proj(10)
                tz = zero_p(CXY[:, :, 0:2])
                x3 = TMP[:, i, :].rearrange("p (n w) -> p n w", n=2)
                t = tt(dve, CXY[:, :, 2:258], pair(b), x3, ALU.mult, t, tm)
                banks.give(b, t)
                tmps.give(i, t)
                j, tfree = tmps.take()
                y = TMP[:, j, :].rearrange("p (n w) -> p n w", n=2)
                for c in range(2):
                    w = lambda tap: small_at("cw", (3 * l + tap) * 2 + c)
                    q = ts(y[:, c, :], CXY[:, c, 0:256], w(0), None, ALU.mult, None, t, tz, tfree)
                    q = stt(y[:, c, :], CXY[:, c, 1:257], w(1), y[:, c, :], ALU.mult, ALU.add, q)
                    q = stt(y[:, c, :], CXY[:, c, 2:258], w(2), y[:, c, :], ALU.mult, ALU.add, q)
                q = tt(dve, y, y, CBG[:, :, :], ALU.mult, q, tk["cbg"])
                tg = gated(2, y, q)
                tmps.give(j, tg)

            def turn_out(name, n, src):
                b, free = banks.take()
                for c in range(2):
                    for q in range(2):
                        tm = tr(b[:, c * 256 + q * P:c * 256 + q * P + P], src[:, q, c * P:c * P + P],
                                oparts[name, 0], oparts[name, 1], free, signal=(c == 1 and q == 1))
                t = gated(n, pair(b), tm)
                banks.give(b, t)

            t_acc = {}

            def branch(n_):
                n = order[n_]
                wh, wl, tw = W.take(("br", l, n), 2, 1024)
                read = []
                for mp in range(4):
                    b, free = banks.take()
                    for j in range(2):
                        m = 2 * mp + j
                        for k in range(2):
                            last = mm3(b[:, 256 * j:256 * j + 256], wh[:, k, m * P:m * P + P], wl[:, k, m * P:m * P + P],
                                       ZH[:, n, k, :], ZL[:, n, k, :], k == 0, k == 1, tw, tk["z", n], free,
                                       signal=(j == 1 and k == 1))
                    msl = M[:, n_ % 2, 2 * mp:2 * mp + 2, :]
                    a = ACC[:, 2 * mp:2 * mp + 2, :]
                    if n_ == 0:
                        t = stt(a, msl, 1.0, pair(b), ALU.add, ALU.mult, last, tk["m", n, mp])
                        banks.give(b, t)
                        read.append(t)
                    else:
                        i, tfree = tmps.take()
                        x = TMP[:, i, :].rearrange("p (n w) -> p n w", n=2)
                        t = stt(x, msl, 1.0, pair(b), ALU.add, ALU.mult, last, tk["m", n, mp], tfree)
                        banks.give(b, t)
                        read.append(t)
                        t = tt(pool, a, a, x, ALU.add, t, t_acc[mp])
                        tmps.give(i, t)
                    t_acc[mp] = t
                W.done(last)
                m_free[n_ % 2] = read

            fl = [lambda i=i: gates(i) for i in (1, 2, 0, 3)]
            fl += [pooling, conv_in]
            for n_ in range(2):
                fl += [lambda n_=n_, j=j: merge(n_, j) for j in range(4)]
                fl.append(lambda n_=n_: branch(n_))
            jobs = [attend_cmp(0), attend_cmp(1)]
            jobs += [attend_causal(k, q) for k in range(3) for q in range(2)]
            run_jobs(jobs, fl)
            turn_out("nsa", 0, ON)
            for j in range(4):
                merge(2, j)
            turn_out("fox", 3, OF)
            branch(2)
            for j in range(4):
                merge(3, j)
            branch(3)
            ta = []
            for mp in range(4):
                s = slice(2 * mp, 2 * mp + 2)
                t = split_from(NH[:, s, 0:256], NL[:, s, 0:256], ACC[:, s, :], None, 0.5, t_acc[mp], t_nread[0])
                ta += [[t], [t]]
            for i in range(4):
                outs = wide(("out", l, i), 8, 256, NH, NL, ta)
                t = tt(dve, X[:, 2 * i:2 * i + 2, 0:256], X[:, 2 * i:2 * i + 2, 0:256], pair(outs[0][0]), ALU.add,
                       outs[1][2], t_xt[2 * i], t_xt[2 * i + 1])
                banks.give(outs[0][0], t)
                t_xt[2 * i] = t_xt[2 * i + 1] = [t]
            t_nread[0] = outs[1][2]
            stack.close()

        gain_in_place("fng")
        W.loads()
        assert sorted(W.keys) == sorted(KEYS) and len(W.used) == len(KEYS)
        for m in range(DT):
            t_out = sp.dma(lambda e, m=m: e.dma_start(out[:, m, :], X[:, m, 0:256]), d_out, t_xt[m])
        end = t_out

        block = ctx.enter_context(nc.Block())

        @block.sync
        def _(e):
            sp.play(e)
            e.wait_ge(*end)

        @block.scalar
        def _(e):
            act.play(e)

        @block.vector
        def _(e):
            dve.play(e)

        @block.gpsimd
        def _(e):
            pool.play(e)

        @block.tensor
        def _(e):
            pe.play(e)




def pack_weights(v):
    w = np.zeros((len(KEYS), P, UNIT), np.float32)

    def put(n, a, nk):
        a = a.reshape(nk, P, a.shape[1]).transpose(1, 0, 2).reshape(P, -1)
        w[n, :, :a.shape[1]] = a

    for n, key in enumerate(KEYS):
        kind, l = key[0], key[1]
        if kind == "ada":
            _, _, g, half = key
            put(n, v["ada_w"][l, 512 * half:512 * half + 512, 512 * g:512 * g + 512], 4)
        elif kind == "qkv":
            put(n, v["a_wqkv" if l == 0 else "b_wqkv"][0, :, 256 * key[2]:256 * key[2] + 256], 8)
        elif kind == "wo":
            put(n, v["a_wo" if l == 0 else "b_wo"][0, :, 256 * key[2]:256 * key[2] + 256], 8)
        elif kind == "up":
            j = key[2]
            u = v["ffn_up"][l]
            put(n, np.concatenate([u[:, P * j:P * j + P], u[:, FF + P * j:FF + P * j + P]], 1), 8)
        elif kind == "down":
            _, _, c, m = key
            put(n, v["ffn_down"][l, 1408 * c:1408 * c + 1408, P * m:P * m + P], 11)
        elif kind == "in":
            cols = in_columns(key[2])
            if key[2] == 3:
                put(n, v["w_in_2"][l][:, cols[:144]], 8)
            else:
                put(n, v["w_in_2"][l][:, cols], 8)
        elif kind == "cmp":
            put(n, v["cmp_w1_2"][l, key[2]], 16)
        elif kind == "br":
            put(n, v["w_branch_2"][l, key[2]], 2)
        elif kind == "out":
            put(n, v["w_out_2"][l, :, 256 * key[2]:256 * key[2] + 256], 8)
    return w


def pack_small(v, late):
    s = np.zeros((P, NSM), np.float32)

    def put(name, a, off=0):
        to, at = (late, LATE) if name in LATE else (s, SM)
        to[:a.shape[0], at[name] + off:at[name] + off + a.shape[1]] = a

    cols = lambda a: np.asarray(a).reshape(-1, P).T
    put("c", cols(v["c"]))
    put("cc", cols(v["c_ctx"]))
    put("adab", cols(v["ada_b"]))
    put("nmix", cols(v["norm_mix"]))
    put("nffn", cols(v["norm_ffn"]))
    put("nout", cols(v["norm_out"]))
    put("fconv", cols(v["ffn_conv"]))
    put("fconvb", cols(v["ffn_conv_b"]))
    put("subln", cols(v["a_subln"]))
    put("normg", cols(v["norm_g_2"]))
    put("foxb", np.tile(v["fox_f_bias_2"].reshape(1, 8), (P, 1)))
    put("cpos", v["cmp_pos_2"].reshape(4, 16, P).transpose(2, 0, 1).reshape(P, 64))
    put("cb1", cols(v["cmp_b1_2"]))
    for l in range(2):
        put("cb2", np.tile(v["cmp_b2_2"][l, 0].reshape(64, 1), (2, 1)), l)
        put("cb2v", np.tile(v["cmp_b2_2"][l, 1].reshape(1, 64), (P, 1)), 64 * l)
        put("w2", np.tile(v["cmp_w2_2"][l, 0], (1, 2)), 2 * l * 128)
        put("w2", v["cmp_w2_2"][l, 1], (2 * l + 1) * 128)
        for c in range(2):
            for g in range(2):
                o = LATE["poolw"] + (2 * l + c) * 128
                late[64 * g:64 * g + 64, o + 64 * g:o + 64 * g + 64] = v["pool_w_2"][l, 2 * c + g]
    put("pscale", cols(v["pool_scale_2"]))
    put("cw", cols(v["conv_w_2"]))
    put("fng", cols(v["final_norm_g_2"]))
    put("lam", np.tile(v["a_lambda"].reshape(1, 256), (P, 1)))
    return s


def pack_rpb(v):
    b = v["b_rpb"][0]
    rows = np.stack([b[:, 7 - r:11 - r, ::-1] for r in range(4)])
    flat = np.zeros(64 + rows.size + 64, np.float32)
    flat[64:64 + rows.size] = rows.ravel()
    return flat


def layout(inputs):
    v = {k: np.asarray(a) for k, a in inputs.items()}
    consts, late = constants()
    small = pack_small(v, late)
    x = np.concatenate([v["x"][0], v["ctx"][0]], 0).T.reshape(DT, P, 512).transpose(1, 0, 2)
    return {
        "wstream": pack_weights(v),
        "small": small,
        "consts": consts,
        "late": late,
        "rpb": pack_rpb(v),
        "xin": np.ascontiguousarray(x),
    }


def kernel(**inputs):
    import concourse.bacc as _bacc
    from concourse.bass_utils import run_bass_kernel_spmd as _run

    arrays = layout(inputs)
    nc = _bacc.Bacc("TRN2", target_bir_lowering=False, num_devices=1, dynamic_dma_scratch_size=1024)
    args = [nc.dram_tensor(n, a.shape, F32, kind="ExternalInput").ap() for n, a in arrays.items()]
    args.append(nc.dram_tensor("out", (P, DT, 256), F32, kind="ExternalOutput").ap())
    bass_two_block_decoder(nc, *args)
    r = _run(nc, [arrays], core_ids=[0])
    got = r.results[0]["out"]
    return np.ascontiguousarray(got.transpose(2, 1, 0)).reshape(1, 256, D)
```

```python
from collections import deque
from contextlib import ExitStack
from functools import partial

import concourse.bass as bass
import numpy as np
from concourse import mybir

F32 = mybir.dt.float32
F32R = mybir.dt.float32r
ALU = mybir.AluOpType
ACT = mybir.ActivationFunctionType
AX = mybir.AxisListType.X

P = 128
D = 1024
DT = 8
FF = 2816
FT = 22
HALF_FT = 11
EPS = 1e-6
NEG = -1e30
LAM_INIT = 0.8 - 0.6 * float(np.exp(-0.3 * 0))

RAW_SLOTS = 3
SPLIT_SLOTS = 3
LOOK = 2
UNIT = 2048
N_TMP = 10
X_BEHIND = (4, 6)
BRANCHES = ("nsa", "pool", "conv", "fox")



def unit_keys():
    keys = []
    for l in range(2):
        keys += [("ada", l, g, half) for g in range(12) for half in range(2)]
        keys += [("qkv", l, i) for i in range(12)]
        keys += [("wo", l, i) for i in range(4)]
        keys += [("up", l, j) for j in range(FT)]
        keys += [("down", l, c, m) for c in range(2) for m in range(DT)]
        keys += [("in", l, i) for i in range(31)]
        keys += [("cmp", l, i) for i in range(2)]
        keys += [("br", l, i) for i in range(4)]
        keys += [("out", l, i) for i in range(4)]
    return keys


KEYS = unit_keys()
UNIT_OF = {k: n for n, k in enumerate(KEYS)}


def in_columns(i):
    r = lambda a, n: list(range(a, a + n))
    if i == 0:
        return r(0, 256)
    if i == 1:
        return r(384, 64) * 2 + r(512, 64) * 2
    if i == 2:
        return r(256, 64) * 2 + r(320, 64) * 2
    if i == 3:
        return r(448, 64) + r(576, 64) + r(640, 12) + r(2444, 4) + [-1] * 112
    if i == 4:
        return r(2188, 256)
    if i == 5:
        return r(1676, 256)
    if i == 6:
        return r(1932, 256)
    if i == 7:
        return r(652, 256)
    if i <= 10:
        return r(908 + 256 * (i - 8), 256)
    if i <= 14:
        return r(2448 + 256 * (i - 11), 256)
    return r(3472 + 256 * (i - 15), 256)




def small_plan():
    at, n = {}, 0
    for name, w in (
        ("c", 8), ("cc", 8), ("adab", 96), ("nmix", 16), ("nffn", 16), ("nout", 8), ("fconv", 264), ("fconvb", 88),
        ("subln", 1), ("normg", 16), ("foxb", 8), ("cpos", 64), ("cb1", 4), ("cb2", 2), ("pscale", 4), ("cw", 12),
        ("fng", 8), ("lam", 256),
    ):
        at[name] = n
        n += w
    return at, n


SM, NSM = small_plan()


def const_plan():
    at, n = {}, 0
    for name, w in (
        ("ident", 128), ("ones", 256), ("c1", 256), ("s1", 256), ("cmpc", 16), ("cmps", 16), ("mna", 64),
        ("cmpadd", 32), ("cmpmul", 32), ("sel", 2), ("mhalf", 1), ("sum16", 16), ("rows", 3),
    ):
        at[name] = n
        n += w
    return at, n


CO, NCO = const_plan()

LATE = {"c2": 0, "s2": 256, "causal": 512, "icnt": 640, "cb2v": 1152, "poolw": 1280, "w2": 1792}
NLATE = 2304


def constants():
    c = np.zeros((P, NCO), np.float32)
    late = np.zeros((P, NLATE), np.float32)
    p = np.arange(P)
    t = np.arange(256)
    f = np.float32

    def put(name, a):
        a = np.asarray(a, np.float32)
        to, at = (late, LATE) if name in LATE else (c, CO)
        to[:, at[name]:at[name] + a.shape[1]] = a

    put("ident", np.eye(P))
    put("ones", np.ones((P, 256)))
    inv = f(10000.0) ** (-np.arange(16, dtype=f) / f(16))
    row, col = (t // 64).astype(f), (t % 64).astype(f)
    d = p % 64
    pos = np.where((d < 32)[:, None], row[None, :], col[None, :]).astype(f)
    ang = (pos * inv[d % 16][:, None]).astype(f)
    sign = np.where(d % 32 < 16, f(-1), f(1))[:, None]
    put("c1", np.cos(ang))
    put("s1", np.sin(ang) * sign)
    inv2 = f(500000.0) ** (-np.arange(8, dtype=f) / f(8))
    sign2 = np.where(d % 16 < 8, f(-1), f(1))[:, None]
    for names, ps in ((("c2", "s2"), t.astype(f)), (("cmpc", "cmps"), (np.arange(16) * 16 + 31).astype(f))):
        a2 = (ps[None, :] * inv2[d % 8][:, None]).astype(f)
        on = (d < 16)[:, None]
        put(names[0], np.where(on, np.cos(a2), 1.0))
        put(names[1], np.where(on, np.sin(a2) * sign2, 0.0))
    put("causal", np.where(p[None, :] <= p[:, None], 0.0, NEG))
    cc = p % 64
    cs = np.clip(cc - 8, 0, 48)
    k = np.arange(64)
    put("mna", np.where((k[None, :] >= cs[:, None]) & (k[None, :] < cs[:, None] + 16), 0.0, NEG))
    n = np.arange(16)
    ok = np.stack([(n[None, :] * 16 + 31 <= (q * 128 + p)[:, None]) & (n < 15)[None, :] for q in range(2)], 1)
    put("cmpadd", np.where(ok, 0.0, NEG).reshape(P, 32))
    put("cmpmul", ok.reshape(P, 32))
    w = np.stack([np.where(p < 64, 2, 4), np.where(p < 64, 8, 16)], 1)
    put("icnt", (f(1) / np.minimum(t[None, None, :] + 1, w[:, :, None]).astype(f)).reshape(P, 512))
    sel = np.zeros((P, 2))
    sel[[0, 2], 0] = 1
    sel[[1, 3], 1] = 1
    put("sel", sel)
    put("sum16", (p[:, None] % 16 == n[None, :]) & (p[:, None] < 32))
    put("rows", np.stack([p % 32 == 0, p % 32 == 1, np.where(p % 32 == 1, -1, 0)], 1))
    put("mhalf", np.full((P, 1), -0.5))
    return c, late




class Lane:

    def __init__(self, sem):
        self.sem, self.n, self.queue = sem, 0, []

    def __call__(self, fn, *waits):
        self.n += 1
        self.queue.append((waits, fn, self.sem, 1))
        return (self.sem, self.n)

    def quiet(self, fn, *waits):
        self.queue.append((waits, fn, None, 0))

    def wait_for(self, tokens):
        self.queue.append(((tokens,), None, None, 0))

    def dma(self, fn, counter, *waits):
        counter[1] += 16
        self.queue.append((waits, fn, counter[0], 16))
        return (counter[0], counter[1])

    def play(self, eng):
        seen = {}

        def wait(w):
            if w is None:
                return
            if isinstance(w, list):
                for x in w:
                    wait(x)
                return
            s, v = w
            if seen.get(s.name, 0) < v:
                eng.wait_ge(s, v)
                seen[s.name] = v

        for waits, fn, sem, n in self.queue:
            wait(list(waits))
            if fn is None:
                continue
            ins = fn(eng)
            if sem is not None:
                ins.then_inc(sem, n)


class Pool:

    def __init__(self, items):
        self.free = deque((x, []) for x in items)

    def take(self):
        return self.free.popleft()

    def give(self, item, *tokens):
        self.free.append((item, list(tokens)))


def bass_two_block_decoder(nc, wstream, small, consts, late, rpb, xin, out):
    ctx = ExitStack()
    with ctx:
        def sb(name, shape, dt=F32, stack=ctx):
            return stack.enter_context(nc.sbuf_tensor(name, shape, dt))

        def new_sem(name):
            return ctx.enter_context(nc.semaphore(name))

        sp, act, dve, pool, pe = (Lane(new_sem(f"s_{n}")) for n in ("sp", "act", "dve", "pool", "pe"))
        d_small, d_const, d_out = ([new_sem(n), 0] for n in ("d_small", "d_const", "d_out"))
        d_late = [new_sem("d_late"), 0]
        d_x = [[new_sem(f"d_x{m}"), 0] for m in range(2)]
        d_raw = [[new_sem(f"d_raw{i}"), 0] for i in range(RAW_SLOTS)]
        d_bias = [[new_sem(f"d_bias{i}"), 0] for i in range(2)]

        banks = Pool([ctx.enter_context(nc.psum_tensor(f"ps{i}", [P, 512], F32)) for i in range(8)])
        SMALL = sb("SMALL", [P, NSM])
        CONST = sb("CONST", [P, NCO])
        X = sb("X", [P, DT, 512])
        RAW = sb("RAW", [P, RAW_SLOTS, UNIT])
        WH = sb("WH", [P, SPLIT_SLOTS, UNIT], F32R)
        WL = sb("WL", [P, SPLIT_SLOTS, UNIT], F32R)
        NH = sb("NH", [P, DT, 512], F32R)
        NL = sb("NL", [P, DT, 512], F32R)
        TMP = sb("TMP", [P, N_TMP, 512])
        CB = sb("CB", [P, 160], F32R)
        CS = sb("CS", [P, 32])
        ADA = sb("ADA", [P, 2, 48, 2])
        AMOD = sb("AMOD", [P, 2, 2, 8, 2])
        MS = sb("MS", [P, 8])
        RS = sb("RS", [P, 8])
        STAT = sb("STAT", [P, 12, 24])
        LAMV = sb("LAMV", [P, 8])
        junk = []
        late_sb = [None]
        tmps = Pool(list(range(N_TMP)))
        stats = Pool(list(range(12)))

        def small_at(name, a, n=1):
            if name in LATE:
                return late_sb[0][:, LATE[name] + a:LATE[name] + a + n]
            return SMALL[:, SM[name] + a:SM[name] + a + n]

        def const_at(name, a=0, n=1):
            if name in LATE:
                return late_sb[0][:, LATE[name] + a:LATE[name] + a + n]
            return CONST[:, CO[name] + a:CO[name] + a + n]

        IDENT = const_at("ident", 0, 128)
        ONE = const_at("ones", 0, 1)

        t_small = sp.dma(lambda e: e.dma_start(SMALL[:, :], small), d_small)
        t_const = (d_const[0], 16)
        t_x = [(d_x[a][0], 16) for a in range(2)]

        def new_scope():
            before = [(q.sem, q.n) for q in (act, dve, pool, pe)]
            for q in (act, dve, pool):
                q.wait_for(before)

        def copy_a(o, i, *w, scale=1.0):
            return act(lambda e: e.activation(o, i, ACT.Copy, scale=scale), *w)

        def activ(o, i, func, *w, **kw):
            return act(lambda e: e.activation(o, i, func, **kw), *w)

        def reduce(o, i, op, negate, *w):
            return dve(lambda e: e.tensor_reduce(o, i, AX, op, negate=negate), *w)

        def recip(o, i, *w):
            return dve(lambda e: e.reciprocal(o, i), *w)

        def zero(o, *w):
            o = o.bitcast(mybir.dt.uint32)
            return dve(lambda e: e.memset(o, 0), *w)

        def zero_p(o, *w):
            return pool(lambda e: e.memset(o, 0.0), *w)

        def scan_sum(o, ones, i, *w):
            return dve(lambda e: e.tensor_tensor_scan(o, ones, i, 0.0, ALU.mult, ALU.add), *w)

        def shuffle(o, i, hop, *w):
            return dve(lambda e: e.stream_shuffle(o, i, hop), *w)

        def copy_v(o, i, *w):
            return dve(lambda e: e.tensor_copy(o, i), *w)

        def tt(lane, o, a, b, op, *w):
            return lane(lambda e: e.tensor_tensor(o, a, b, op), *w)

        def ts(o, a, s1, s2, op0, op1, *w):
            if s2 is None:
                return dve(lambda e: e.tensor_scalar(o, a, s1, None, op0), *w)
            return dve(lambda e: e.tensor_scalar(o, a, s1, s2, op0, op1), *w)

        def stt(o, a, s, b, op0, op1, *w):
            return dve(lambda e: e.scalar_tensor_tensor(out=o, in0=a, scalar=s, in1=b, op0=op0, op1=op1), *w)

        def mm(o, l, r, start, stop, *w, signal=False, loose=False):
            fn = lambda e: e.matmul(o, l, r, start=start, stop=stop, skip_group_check=loose)
            return pe(fn, *w) if signal else pe.quiet(fn, *w)

        def mm3(o, lh, ll, rh, rl, start, stop, *w, signal=False):
            mm(o, lh, rh, start, False, *w)
            mm(o, lh, rl, False, False)
            return mm(o, ll, rh, False, stop, signal=signal)

        def tr(o, i, *w, signal=False):
            fn = lambda e: e.transpose(o, i, IDENT)
            return pe(fn, *w) if signal else pe.quiet(fn, *w)

        class Weights:
            def __init__(self):
                self.keys, self.low, self.used, self.made = [], [], [], 0
                self.high, self.shape, self.pool_every = [], [], 1000
                for _ in range(LOOK):
                    self.prepare()

            def prepare(self):
                v = self.made
                if v >= len(KEYS):
                    return
                self.made += 1
                loaded = (d_raw[v % RAW_SLOTS][0], 16 * (v // RAW_SLOTS + 1))
                last_use = self.used[v - SPLIT_SLOTS] if v >= SPLIT_SLOTS else None
                raw = RAW[:, v % RAW_SLOTS, :]
                s = v % SPLIT_SLOTS
                cut = lambda h: slice(self.ends(v)[h], self.ends(v)[h + 1])
                self.high.append([act(
                    lambda e, h=h: e.activation(WH[:, s, cut(h)], raw[:, cut(h)], ACT.Copy), loaded, last_use)
                    for h in range(2)])
                low = []
                for h in range(2):
                    lane = pool if h == 1 and v % self.pool_every == 0 else dve
                    low.append(lane(
                        lambda e, h=h: e.tensor_tensor(WL[:, s, cut(h)], raw[:, cut(h)],
                                                       WH[:, s, cut(h)].bitcast(F32), ALU.subtract),
                        self.high[v][h]))
                self.low.append(low)

            def ends(self, v):
                nk, n = self.shape[v]
                return 0, (nk + 1) // 2 * n, nk * n

            def take(self, key, nk, nc_):
                v = len(self.keys)
                self.keys.append(key)
                self.shape.append((nk, nc_))
                self.prepare()
                s = v % SPLIT_SLOTS
                view = lambda t: t[:, s, 0:nk * nc_].rearrange("p (k n) -> p k n", k=nk)
                ready = [[self.high[v][h], self.low[v][h]] for h in range(2)]
                return view(WH), view(WL), [ready[0] if k < (nk + 1) // 2 else ready[1] for k in range(nk)]

            def done(self, token):
                self.used.append(token)

            def loads(self):
                for v, key in enumerate(self.keys):
                    n = UNIT_OF[key]
                    free = self.low[v - RAW_SLOTS] if v >= RAW_SLOTS else None
                    size = self.ends(v)[2]
                    sp.dma(lambda e, v=v, n=n, size=size: e.dma_start(
                        RAW[:, v % RAW_SLOTS, 0:size], wstream[n, :, 0:size]), d_raw[v % RAW_SLOTS], free)
                    if v == 1:
                        sp.dma(lambda e: e.dma_start(CONST[:, :], consts), d_const)
                    if v in X_BEHIND:
                        a = X_BEHIND.index(v)
                        sp.dma(lambda e, a=a: e.dma_start(X[:, 4 * a:4 * a + 4, :], xin[:, 4 * a:4 * a + 4, :]), d_x[a])

        t = zero(CB[:, 32:160])
        t_cb0 = t
        cs = CS[:, 0:16]
        t = activ(cs, small_at("c", 0, 16), ACT.Silu, t_small)
        csv = cs.rearrange("p (v k) -> p k v", v=2)
        cbv = CB[:, 0:32].rearrange("p (k s v) -> p k s v", k=8, s=2)
        t1 = copy_v(cbv[:, :, 0, :], csv, t)
        t_cb = [t_cb0, tt(dve, cbv[:, :, 1, :], csv, cbv[:, :, 0, :].bitcast(F32), ALU.subtract, t1)]

        W = Weights()
        pending = []
        t_ada = {}

        def ada_group(l, g):
            b, free = banks.take()
            for half in range(2):
                wh, wl, tw = W.take(("ada", l, g, half), 4, 512)
                for k in range(4):
                    kk = 4 * half + k
                    lhs = CB[:, 4 * kk:4 * kk + P]
                    mm(b[:, :], lhs, wh[:, k, :], kk == 0, False, tw[k], t_cb, free)
                    last = mm(b[:, :], lhs, wl[:, k, :], False, kk == 7, signal=(k == 3))
                W.done(last)
            r, rfree = tmps.take()
            tc = copy_a(TMP[0:4, r, :], b[0:4, :], last, rfree)
            banks.give(b, tc)
            pending.append((l, g, r, tc))
            if len(pending) > 1:
                ada_finish()

        def ada_finish():
            l, g, r, tc = pending.pop(0)
            b, free = banks.take()
            for j in range(4):
                last = mm(b[:, 2 * j:2 * j + 2], TMP[0:4, r, P * j:P * j + P], CONST[0:4, CO["sel"]:CO["sel"] + 2],
                          True, True, tc, t_const, free, signal=(j == 3))
            tmps.give(r, last)
            bias = small_at("adab", 48 * l + 4 * g, 4).unsqueeze(2).to_broadcast([P, 4, 2])
            td = tt(dve, ADA[:, l, 4 * g:4 * g + 4, :], b[:, 0:8].rearrange("p (j v) -> p j v", v=2), bias, ALU.add,
                    last, t_small)
            banks.give(b, td)
            t_ada[l, g] = td

        def ada_param(l, p, m, v):
            return ADA[:, l, 8 * p + m, v:v + 1]

        def ada_tokens(l, p):
            return [t_ada[l, 2 * p], t_ada[l, 2 * p + 1]]

        def gain(l, which):
            p = 1 if which == 0 else 4
            g = small_at("nmix" if which == 0 else "nffn", 8 * l, 8).unsqueeze(2).to_broadcast([P, 8, 2])
            return stt(AMOD[:, l, which, :, :], ADA[:, l, 8 * p:8 * p + 8, :], 1.0, g, ALU.add, ALU.mult,
                       ada_tokens(l, p))

        t_ms = [None]
        t_rs = [None]
        t_rsread = [None]

        class Rms:

            def __init__(self, T):
                self.T, self.nt, self.at, self.summed, self.squares = T, T // P, 0, 0, []
                self.b, self.free = banks.take()

            def square(self, upto=DT, lanes=1):
                while self.at < upto:
                    i, tfree = tmps.take()
                    sq, x = TMP[:, i, 0:self.T], X[:, self.at, 0:self.T]
                    if self.at % 2 == 1 and lanes == 2:
                        t = tt(dve, sq, x, x, ALU.mult, t_xt[self.at], tfree)
                    else:
                        t = activ(sq, x, ACT.Square, t_xt[self.at], tfree)
                    self.squares.append((i, t))
                    self.at += 1

            def sums(self):
                for i, ta in self.squares:
                    m = self.summed
                    for q in range(self.nt):
                        self.last = mm(self.b[:, q:q + 1], TMP[:, i, q * P:q * P + P], ONE, m == 0 and q == 0,
                                       m == DT - 1, ta, t_const, self.free, signal=(q == self.nt - 1), loose=True)
                    tmps.give(i, self.last)
                    self.summed += 1
                self.squares = []

            def finish(self, fill=()):
                self.square()
                self.sums()
                b, nt, last = self.b, self.nt, self.last
                td = ts(MS[:, 0:nt], b[:, 0:nt], 1.0 / D, EPS, ALU.mult, ALU.add, last, t_rs[0])
                banks.give(b, td)
                tp = tt(pool, RS[:, 0:nt], MS[:, 0:nt], const_at("mhalf").to_broadcast([P, nt]), ALU.pow, td, t_rsread[0])
                t_rs[0] = tp
                if fill:
                    every, W.pool_every = W.pool_every, 1
                    fill.pop(0)()
                    W.pool_every = every
                b, free = banks.take()
                for q in range(nt):
                    last = mm(b[:, q * P:q * P + P], RS[:, q:q + 1].to_broadcast([P, P]), IDENT, True, True, tp, free,
                              signal=(q == nt - 1))
                t_rsread[0] = last
                return b, last

        t_nread = [None]

        def norm_split(T, stats_, scale, shift, tpar, fill=()):
            b, tb = stats_
            out_t = []
            halves = [(0, 0, 256)] if T == 256 else [(0, 0, 256), (1, 256, 512)]
            scaled = deque()

            def begin(m):
                i, tfree = tmps.take()
                for v, a, z in halves:
                    t1 = stt(TMP[:, i, a:z], X[:, m, a:z], scale(m, v), b[:, a:z], ALU.mult, ALU.mult, tb, tpar, tfree)
                    scaled.append((m, i, v, TMP[:, i, a:z], NH[:, m, a:z], NL[:, m, a:z], t1))
                return t1

            def end():
                got = []
                for _ in halves:
                    m, i, v, x, nh, nl, t1 = scaled.popleft()
                    if shift is None:
                        t2 = copy_a(nh, x, t1, t_nread[0])
                        got.append((pool if m % 2 else dve, x, nh, nl, None, t2))
                        continue
                    sh = shift(m, v)
                    t2 = activ(nh, x, ACT.Identity, t1, t_nread[0], bias=sh)
                    if m % 2:
                        t2 = activ(x, x, ACT.Identity, t2, bias=sh)
                        sh = None
                    got.append((pool if m % 2 else dve, x, nh, nl, sh, t2))
                toks = []
                for lane, x, nh, nl, sh, t2 in got:
                    if sh is None:
                        toks.append(tt(lane, nl, x, nh.bitcast(F32), ALU.subtract, t2))
                    else:
                        toks.append(stt(nl, x, sh, nh.bitcast(F32), ALU.add, ALU.subtract, t2))
                tmps.give(i, toks)
                out_t.append(toks)

            begin(0)
            for m in range(DT):
                if m + 1 < DT:
                    t1 = begin(m + 1)
                end()
                if fill and m % 2 == 1:
                    fill.pop(0)()
            while fill:
                fill.pop(0)()
            banks.give(b, t1)
            return out_t

        def wide(key, nk, T, xh, xl, tx, t0=0, abreast=False):
            wh, wl, tw = W.take(key, nk, 256)
            outs = []
            if T == 256:
                b, free = banks.take()
                outs = [(b, b[:, 0:256], free), (b, b[:, 256:512], free)]
            else:
                for _ in range(2):
                    b, free = banks.take()
                    outs.append((b, b[:, :], free))
            if abreast:
                last = [None, None]
                for k in range(nk):
                    for j, (b, o, free) in enumerate(outs):
                        last[j] = mm3(o, wh[:, k, P * j:P * j + P], wl[:, k, P * j:P * j + P], xh[:, k, t0:t0 + T],
                                      xl[:, k, t0:t0 + T], k == 0, k == nk - 1, tw[k], tx[k], free,
                                      signal=(k == nk - 1))
                W.done(last[1])
                return [(b, o, last[j]) for j, (b, o, free) in enumerate(outs)]
            for j, (b, o, free) in enumerate(outs):
                for k in range(nk):
                    last = mm3(o, wh[:, k, P * j:P * j + P], wl[:, k, P * j:P * j + P], xh[:, k, t0:t0 + T],
                               xl[:, k, t0:t0 + T], k == 0, k == nk - 1, tw[k], tx[k], free, signal=(k == nk - 1))
                outs[j] = (b, o, last)
            W.done(last)
            return outs

        def tall(key, n, nt, tx):
            wh, wl, tw = W.take(key, 8, 256 if n == 256 else n)
            res = []
            for q in range(nt):
                if q % 2 == 0:
                    b, free = banks.take()
                o = b[:, 256 * (q % 2):256 * (q % 2) + n]
                for k in range(8):
                    c = slice(q * P, q * P + P)
                    last = mm3(o, NH[:, k, c], NL[:, k, c], wh[:, k, 0:n], wl[:, k, 0:n], k == 0, k == 7,
                               tw[k], tx[k], free, signal=(k == 7))
                if q % 2 == 1:
                    res.append((b, last))
            W.done(last)
            return res

        def rotate(o, src, tsrc, C, S, scale, bank=None):
            n, w = src.shape[1], src.shape[2]
            i, f1 = tmps.take()
            j, f2 = tmps.take()
            a = TMP[:, i, 0:n * w].rearrange("p (n w) -> p n w", n=n)
            s = TMP[:, j, 0:n * w].rearrange("p (n w) -> p n w", n=n)
            Cb, Sb = (q.unsqueeze(1).to_broadcast([P, n, w]) for q in (C, S))
            ta = copy_a(a, src, tsrc, f1, scale=scale)
            hop = w_hop[0]
            tb = shuffle(s, a, hop, ta, f2)
            tc = tt(pool, o, a, Cb, ALU.mult, ta, t_const)
            td = tt(dve, s, s, Sb, ALU.mult, tb, t_const)
            te = tt(dve, o, o, s, ALU.add, tc, td)
            tmps.give(i, [tb, tc])
            tmps.give(j, te)
            return ta, te

        w_hop = [None]

        def split_from(oh, ol, src, scale_ap, scale, tsrc, *w):
            s = scale_ap if scale_ap is not None else scale
            ta = activ(oh, src, ACT.Copy, tsrc, *w, scale=s)
            tb = stt(ol, src, s, oh.bitcast(F32), ALU.mult, ALU.subtract, ta, *w)
            return tb

        def run_jobs(jobs, fillers, steps=None):
            jobs, fillers, live, n = deque(jobs), deque(fillers), deque(), 0
            while jobs or live:
                for g in list(live):
                    try:
                        next(g)
                    except StopIteration:
                        live.remove(g)
                if jobs:
                    g = jobs.popleft()
                    next(g)
                    live.append(g)
                n += 1
                if fillers and (steps is None or n in steps):
                    fillers.popleft()()
            while fillers:
                fillers.popleft()()

        t_xt = [[t_x[m // 4]] for m in range(DT)]

        def attend_diff(h, qt, Q, K, V, tqk, tv, O, tofree, done, SS):
            k0 = 0 if qt < 2 else 256
            nk = 512 - k0
            st, sfree = stats.take()
            nm, sm, r, ratio = (STAT[:, st, 2 * i:2 * i + 2] for i in range(4))
            pt, sc = [], []
            for j in range(2):
                b, free = banks.take()
                ps = slice(64 * j, 64 * j + 64)
                tm = mm(b[:, 0:nk], Q[ps, h, qt * P:qt * P + P], K[ps, h, k0:512], True, True, tqk, free, signal=True)
                sc.append((b, tm))
            yield
            for j, (b, tm) in enumerate(sc):
                t1 = reduce(nm[:, j:j + 1], b[:, 0:nk], ALU.max, True, tm, sfree)
                i, tfree = tmps.take()
                t2 = activ(TMP[:, i, 0:nk], b[:, 0:nk], ACT.Exp, t1, tfree, bias=nm[:, j:j + 1], accum_out=sm[:, j:j + 1])
                banks.give(b, t2)
                pt.append((i, t2))
            yield
            t3 = recip(r, sm, pt[0][1], pt[1][1], sfree)
            t4 = stt(ratio[:, 0:1], sm[:, 0:1], r[:, 1:2], LAMV[:, 0:1], ALU.mult, ALU.mult, t3, t_lam)
            (i0, ta), (i1, tb) = pt
            p0, p1 = TMP[:, i0, 0:nk], TMP[:, i1, 0:nk]
            if qt == 1:
                t5 = tt(pool, p1, p1, ratio[:, 0:1].to_broadcast([P, nk]), ALU.mult, t4, tb)
                t5 = tt(pool, p0, p0, p1, ALU.add, t5, ta)
            else:
                t5 = stt(p0, p1, ratio[:, 0:1], p0, ALU.mult, ALU.add, t4, ta, tb)
            tmps.give(i1, t5)
            yield
            b, free = banks.take()
            for k in range(nk // P):
                tm = tr(b[:, k * P:k * P + P], TMP[:, i0, k * P:k * P + P], t5, free, signal=(k == nk // P - 1))
            tmps.give(i0, tm)
            i, tfree = tmps.take()
            te = copy_a(TMP[:, i, 0:nk], b[:, 0:nk], tm, tfree)
            banks.give(b, te)
            yield
            yield
            b, free = banks.take()
            for k in range(nk // P):
                tm = mm(b[:, 0:P], TMP[:, i, k * P:k * P + P], V[:, k0 // P + k, h * P:h * P + P], k == 0,
                        k == nk // P - 1, te, tv, free, signal=(k == nk // P - 1))
            tmps.give(i, tm)
            yield
            t5 = ts(TMP[:, O, qt * P:qt * P + P], b[:, 0:P], r[:, 0:1], None, ALU.mult, None, tm, t3, tofree)
            banks.give(b, t5)
            stats.give(st, t5)
            yield
            t6 = activ(junk[0][:, :], TMP[:, O, qt * P:qt * P + P], ACT.Square, t5, SS[1], t_junk[0],
                       accum_out=SS[0][:, qt:qt + 1])
            t_junk[0] = t6
            done.append(t6)
            if qt == 3:
                yield
                ms, rs = SS[0][:, 8:12], SS[0][:, 16:20]
                t7 = ts(ms, SS[0][:, 0:4], 1.0 / P, EPS, ALU.mult, ALU.add, done)
                t8 = tt(pool, rs, ms, const_at("mhalf").to_broadcast([P, 4]), ALU.pow, t7, t_const)
                yield
                o4 = TMP[:, O, :].rearrange("p (q w) -> p q w", q=4)
                t9 = tt(dve, o4, o4, rs.unsqueeze(2).to_broadcast([P, 4, P]), ALU.mult, t8)
                stats.give(SS[2], t9)
                yield
                b, free = banks.take()
                for q in range(4):
                    tm = tr(b[:, q * P:q * P + P], TMP[:, O, q * P:q * P + P], t9, free, signal=(q == 3))
                tmps.give(O, tm)
                tl = split_from(NH[:, h, :], NL[:, h, :], b[:, :], LAMV[:, 1:2], None, tm, t_lam, t_nread[0])
                banks.give(b, tl)
                t_o[h] = tl

        t_o = {}
        t_junk = [None]

        def attend_na(h, qt, Q, K, V, tqk, tv, bias, tbias, O, tofree, done, bias_done):
            m, e2 = h // 2, h % 2
            st, sfree = stats.take()
            nm, sm, r = (STAT[:, st, i:i + 1] for i in range(3))
            b, free = banks.take()
            ps = slice(64 * e2, 64 * e2 + 64)
            tm = mm(b[:, :], Q[ps, m, qt * P:qt * P + P], K[ps, m, :], True, True, tqk, free, signal=True)
            yield
            t0 = tt(dve, b[:, 0:256], b[:, 0:256], bias, ALU.add, tm, tbias)
            bias_done.append(t0)
            t1 = reduce(nm, b[:, :], ALU.max, True, t0, sfree)
            i0, tfree = tmps.take()
            t2 = activ(TMP[:, i0, :], b[:, :], ACT.Exp, t1, tfree, bias=nm, accum_out=sm)
            banks.give(b, t2)
            yield
            yield
            b, free = banks.take()
            for k in range(4):
                tm = tr(b[:, k * P:k * P + P], TMP[:, i0, k * P:k * P + P], t2, free, signal=(k == 3))
            tmps.give(i0, tm)
            i, tfree = tmps.take()
            te = copy_a(TMP[:, i, :], b[:, :], tm, tfree)
            banks.give(b, te)
            yield
            yield
            b, free = banks.take()
            for k in range(4):
                tm = mm(b[:, 0:64], TMP[:, i, k * P:k * P + P], V[:, k, h * 64:h * 64 + 64], k == 0, k == 3, te, tv,
                        free, signal=(k == 3))
            tmps.give(i, tm)
            yield
            c = qt * P + e2 * 64
            t3 = recip(r, sm, t2, sfree)
            t4 = ts(TMP[:, O, c:c + 64], b[:, 0:64], r, None, ALU.mult, None, tm, t3, tofree)
            banks.give(b, t4)
            stats.give(st, t4)
            done.append(t4)
            yield
            if len(done) == 4:
                yield
                b, free = banks.take()
                for q in range(2):
                    tm = tr(b[:, q * P:q * P + P], TMP[:, O, q * P:q * P + P], done, free, signal=(q == 1))
                tmps.give(O, tm)
                tl = split_from(NH[:, m, 0:256], NL[:, m, 0:256], b[:, 0:256], None, 1.0, tm, t_nread[0])
                banks.give(b, tl)
                t_o[m] = tl

        def residual(outs, m0, T, gate, tg):
            for j, (b, o, tm) in enumerate(outs):
                m = m0 + j
                for v in range(T // 256):
                    c = slice(256 * v, 256 * v + 256)
                    t = stt(X[:, m, c], o[:, c], gate(m, v), X[:, m, c], ALU.mult, ALU.add, tm, tg, t_xt[m], t_xr)
                t_xt[m] = [t]
            for b in {id(o[0]): o[0] for o in outs}.values():
                banks.give(b, t)

        t_xr = []
        fill = deque()

        def fillers(n):
            for _ in range(n):
                if fill:
                    fill.popleft()()

        def ffn(l, T, tn):
            stack = ExitStack()
            nch = 2 if T == 512 else 1
            nj = FT // nch
            HH = sb(f"HH{l}", [P, nj, T], F32R, stack)
            HL = sb(f"HL{l}", [P, nj, T], F32R, stack)
            ns = T // 256
            t_hread = None
            tail = lambda: None

            def gate_up(acc, hh, hl, th, tfree):
                (ia, aa, _, _, ta, _, _), (ig, ag, _, _, tg, _, _) = acc
                t4 = activ(ag, ag, ACT.Silu, tg)
                t5 = tt(dve, aa, aa, ag, ALU.mult, t4, ta)
                tmps.give(ig, t5)
                t6 = (copy_v if T == 256 else copy_a)(hh, aa, t5, tfree)
                t7 = tt(pool, hl, aa, hh.bitcast(F32), ALU.subtract, t6)
                tmps.give(ia, t7)
                th.append([t6, t7])

            for c in range(nch):
                W.pool_every = 2 if T == 512 else 1000
                th = []
                for jj in range(nj):
                    j = c * nj + jj
                    outs = wide(("up", l, j), 8, T, NH, NL, tn, abreast=(j == 0 and T == 512))
                    tail()
                    acc = []
                    for s, (b, o, tm) in enumerate(outs):
                        col = 44 * l + j + FT * s
                        w = lambda tap, j=j, s=s: small_at("fconv", (3 * l + tap) * 44 + j + FT * s)
                        i, tfree = tmps.take()
                        a = TMP[:, i, 0:T]
                        a3 = a.rearrange("p (n w) -> p n w", n=ns)
                        o3 = o.rearrange("p (n w) -> p n w", n=ns)
                        if T == 256:
                            tm = outs[1][2]
                        t1 = activ(a, o, ACT.Identity, tm, tfree, scale=w(1), bias=small_at("fconvb", col))
                        acc.append([i, a, a3, o3, t1, w, b])
                    for s in range(2):
                        i, a, a3, o3, t1, w, b = acc[s]
                        first = [acc[0][4], acc[1][4]] if T == 256 else t1
                        t2 = stt(a3[:, :, 1:256], o3[:, :, 0:255], w(0), a3[:, :, 1:256], ALU.mult, ALU.add, first)
                        t3 = stt(a3[:, :, 0:255], o3[:, :, 1:256], w(2), a3[:, :, 0:255], ALU.mult, ALU.add, t2)
                        acc[s][4] = t3
                        if T != 256:
                            banks.give(b, t3)
                    if T == 256:
                        banks.give(b, t3)
                    if j == 5:
                        ada_group(1, 3 if l == 0 else 11)
                    tail = partial(gate_up, acc, HH[:, jj, :], HL[:, jj, :], th, t_hread)
                t_nread[0] = outs[1][2]
                tail()
                tail = lambda: None
                while pending:
                    ada_finish()
                if c == nch - 1:
                    R = Rms(T)
                for m in range(DT):
                    b, free = banks.take()
                    for half in range(nj // HALF_FT):
                        wh, wl, tw = W.take(("down", l, c if nch == 2 else half, m), HALF_FT, 128)
                        for k in range(HALF_FT):
                            kk = half * HALF_FT + k
                            last = mm3(b[:, 0:T], wh[:, k, :], wl[:, k, :], HH[:, kk, :], HL[:, kk, :], kk == 0,
                                       kk == nj - 1, tw[k], th[kk], free, signal=(k == HALF_FT - 1))
                        W.done(last)
                    if c == nch - 1:
                        R.sums()
                    residual([(b, b[:, 0:T], last)], m, T, lambda m, v: ada_param(l, 5, m, v), ada_tokens(l, 5))
                    if c == nch - 1:
                        R.square(m + 1)
                t_hread = last
            stack.close()
            return R

        lamv = lambda a, n: SMALL[:, SM["lam"] + a:SM["lam"] + a + n]
        tl1 = tt(dve, LAMV[:, 4:5].to_broadcast([P, 1]), small_at("subln", 0), ONE, ALU.bypass, t_small, t_const)
        i, tfree = tmps.take()
        tl = []
        for j in range(2):
            t = tt(dve, TMP[:, i, 64 * j:64 * j + 64], lamv(128 * j, 64), lamv(128 * j + 64, 64), ALU.mult, t_small)
            tl.append(reduce(LAMV[:, 2 + j:3 + j], TMP[:, i, 64 * j:64 * j + 64], ALU.add, False, t))
        tmps.give(i, tl)
        t = activ(LAMV[:, 4:6], LAMV[:, 2:4], ACT.Exp, tl, tl1)
        t = tt(dve, LAMV[:, 6:7], LAMV[:, 5:6], LAMV[:, 4:5], ALU.subtract, t)
        t1 = ts(LAMV[:, 0:1], LAMV[:, 6:7], -LAM_INIT, None, ALU.add, None, t)
        t2 = ts(LAMV[:, 1:2], small_at("subln", 0), 1.0 - LAM_INIT, None, ALU.mult, None, t_small)
        t_lam = [t1, t2]

        for g in range(3):
            ada_group(0, g)
        R = Rms(512)
        R.square(6, 2)
        ada_group(0, 3)
        R.sums()
        R.square(DT, 2)
        first = R.finish([lambda: None])
        while pending:
            ada_finish()
        groups = lambda l, a, z: [lambda g=g: ada_group(l, g) for g in range(a, z)]

        for l in range(2):
            Tq = 512 if l == 0 else 256
            tg = gain(l, 0)
            t_am = [tg, ada_tokens(l, 0)]
            spare = [] if l == 0 else groups(1, 4, 5)
            stats_ = first if l == 0 else R.finish(spare)
            tn = norm_split(512, stats_, lambda m, v: AMOD[:, l, 0, m, v:v + 1], lambda m, v: ada_param(l, 0, m, v),
                            t_am, spare)
            stack = ExitStack()
            new_scope()
            Q = sb(f"Q{l}", [P, DT, Tq], F32, stack)
            K = sb(f"K{l}", [P, DT, 512], F32, stack)
            V = sb(f"V{l}", [P, 4, D], F32, stack)
            if l == 0:
                junk.append(sb("JUNK", [P, P], F32, stack))
            if l == 1:
                BI = sb("BI", [P, 2, 2, 16, 64], F32, stack)
                BR = sb("BR", [P, 2, 2, 16, 64], F32, stack)
                t_bfree = {0: [], 1: []}
                t_b = {}
                t_rev = [None, None]

                def load_bias(ch):
                    s = ch % 2
                    for r in range(4):
                        base = 64 + ((r * 16 + 4 * ch) * 4) * 31 + 15 - 63
                        src = bass.AP(rpb.tensor, base, [[1, 64], [31, 16], [1, 64]])
                        p0 = 64 * (r % 2)
                        t = act.dma(lambda e, s=s, r=r, src=src, p0=p0: e.dma_start(
                            BR[p0:p0 + 64, s, r // 2, :, :], src), d_bias[s], t_rev[s])
                    rev = bass.AP(BR[:, :, :, :, :].tensor, 2048 * s + 63, [[4096, P], [64, 32], [-1, 64]])
                    v = BI[:, s, :, :, :].rearrange("p a r c -> p (a r) c")
                    t_b[ch] = tt(pool, v, rev, const_at("mna", 0, 64).unsqueeze(1).to_broadcast([P, 32, 64]), ALU.add,
                                 t, t_bfree[s])
                    t_rev[s] = t_b[ch]

                load_bias(0)
                load_bias(1)
            hop = [16 + i for i in range(16)] + list(range(16))
            w_hop[0] = hop
            tqk = {}
            W.pool_every = 2 if l == 0 else 1000
            rest = groups(0, 4, 8) if l == 0 else groups(1, 5, 6)
            for n_, i in enumerate(range(8) if l == 0 else (4, 5, 6, 7, 0, 1, 2, 3)):
                isq = i < 4
                T = Tq if isq else 512
                outs = wide(("qkv", l, i), 8, T, NH, NL, tn, abreast=(n_ == 0))
                dst = Q if isq else K
                scale = 0.125 if isq else 1.0
                if T == 256:
                    m = 2 * i
                    t = copy_a(dst[:, m:m + 2, :], outs[0][0][:, :].rearrange("p (n w) -> p n w", n=2), outs[1][2],
                               scale=scale)
                    banks.give(outs[0][0], t)
                    tqk["q", m] = tqk["q", m + 1] = [t]
                else:
                    for j, (b, o, tm) in enumerate(outs):
                        m = 2 * (i % 4) + j
                        if l == 0:
                            tc = copy_a(dst[:, m, 256:512], o[:, 256:512], tm, scale=scale)
                            ta, te = rotate(dst[:, m:m + 1, 0:256], o[:, 0:256].unsqueeze(1), tm,
                                            const_at("c1", 0, 256), const_at("s1", 0, 256), scale)
                            banks.give(b, [tc, ta])
                            tqk["q" if isq else "k", m] = [tc, te]
                        else:
                            tc = copy_a(dst[:, m, :], o, tm, scale=scale)
                            banks.give(b, tc)
                            tqk["k", m] = [tc]
                if rest and i % 2 == 1:
                    rest.pop(0)()
            tv = []
            W.pool_every = 1
            for i in range(4):
                for q, (b, tm) in enumerate(tall(("qkv", l, 8 + i), 256, 4, tn)):
                    t = copy_a(V[:, 2 * q:2 * q + 2, 256 * i:256 * i + 256],
                               b[:, :].rearrange("p (n w) -> p n w", n=2), tm)
                    banks.give(b, t)
                tv.append(t)
                t_nread[0] = tm
            if l == 0:
                jobs = []
                fl = groups(0, 8, 12) + groups(1, 0, 2)
                for h in range(DT):
                    holder = {}

                    def job(h, qt, holder):
                        if qt == 0:
                            holder["O"], holder["free"] = tmps.take()
                            holder["done"] = []
                            st, sfree = stats.take()
                            holder["ss"] = STAT[:, st, :], sfree, st
                        yield from attend_diff(h, qt, Q, K, V, [tqk["q", h], tqk["k", h]], tv, holder["O"],
                                               holder["free"], holder["done"], holder["ss"])

                    jobs += [job(h, qt, holder) for qt in (0, 2, 1, 3)]
                run_jobs(jobs, fl, (10, 20, 34, 37, 39, 41))
            else:
                bias_done = {c: [] for c in range(4)}
                jobs = []

                def job(m, qt, e2, holder):
                    if "O" not in holder:
                        holder["O"], holder["free"] = tmps.take()
                        holder["done"] = []
                    h = 2 * m + e2
                    ch = h // 4
                    if h % 4 == 0 and qt == 0 and ch in (1, 2):
                        t_bfree[(ch + 1) % 2] = list(bias_done[ch - 1])
                        load_bias(ch + 1)
                    bias = BI[:, ch % 2, qt, 4 * (h % 4):4 * (h % 4) + 4, :]
                    yield from attend_na(h, qt, Q, K, V, [tqk["q", m], tqk["k", m]], tv,
                                         bias.rearrange("p r c -> p (r c)"), t_b[ch], holder["O"], holder["free"],
                                         holder["done"], bias_done[ch])

                for m in range(DT):
                    holder = {}
                    jobs += [job(m, qt, e2, holder) for qt in range(2) for e2 in range(2)]
                run_jobs(jobs, groups(1, 6, 10), (12, 24, 34, 38))
            stack.close()
            W.pool_every = 1000
            if l == 1:
                late_sb[0] = sb("LATEC", [P, NLATE])
                before = [(q.sem, q.n) for q in (act, dve, pool, pe)]
                t_late = act.dma(lambda e: e.dma_start(late_sb[0][:, :], late), d_late, before)
            to = [[t_o[m]] for m in range(DT)]
            R = Rms(Tq)
            for i in range(4):
                outs = wide(("wo", l, i), 8, Tq, NH, NL, to, abreast=(i == 0 and Tq == 512))
                if Tq == 256:
                    outs[0] = (outs[0][0], outs[0][1], outs[1][2])
                R.sums()
                residual(outs, 2 * i, Tq, lambda m, v: ada_param(l, 2, m, v), ada_tokens(l, 2))
                R.square(2 * i + 2)
                while pending:
                    ada_finish()
            t_nread[0] = outs[1][2]
            tg = gain(l, 1)
            t_am = [tg, ada_tokens(l, 3)]
            spare = groups(1, 2, 3) if l == 0 else groups(1, 10, 11)
            tn = norm_split(Tq, R.finish(spare), lambda m, v: AMOD[:, l, 1, m, v:v + 1],
                            lambda m, v: ada_param(l, 3, m, v), t_am, spare)
            R = ffn(l, Tq, tn)
            W.pool_every = 1000

        def gain_in_place(name, R):
            b, tb = R.finish()
            for m in range(DT):
                t = stt(X[:, m, 0:256], X[:, m, 0:256], small_at(name, m), b[:, 0:256], ALU.mult, ALU.mult, tb, t_xt[m])
                t_xt[m] = [t]
            banks.give(b, t)

        gain_in_place("nout", R)
        W.pool_every = 1

        for q in (dve, pool, act, pe):
            q.wait_for([t_late])
        for l in range(2):
            if l == 0:
                R = Rms(256)
            tn = norm_split(256, R.finish(), lambda m, v: small_at("normg", 8 * l + m), None, t_small)
            stack = ExitStack()
            new_scope()
            mk = lambda name, shape, dt=F32: sb(f"{name}_{l}", shape, dt, stack)
            QN, KN = mk("QN", [P, 2, 256]), mk("KN", [P, 2, 256])
            KC = mk("KC", [P, 2, 256])
            VN = mk("VN", [P, 2, 144])
            VF = mk("VF", [P, 2, 256])
            QF, KF = mk("QF", [P, 2, 256]), mk("KF", [P, 2, 256])
            PU = mk("PU", [P, 2, 2, 272])
            CXY = mk("CXY", [P, 2, 258])
            CBG = mk("CBG", [P, 2, 256])
            G = mk("G", [P, 8, 256])
            M = mk("M", [P, 2, 8, 256])
            LF = mk("LF", [P, 2, 128])
            CR = mk("CR", [P, 256])
            NCR = mk("NCR", [P, 256])
            ON = mk("ON", [P, 2, 256])
            OF = mk("OF", [P, 2, 256])
            ZH, ZL = (t[:, :, 256:512].rearrange("p (n k) w -> p n k w", n=4) for t in (NH, NL))
            ACC = X[:, :, 256:512]
            iflt, t_flt = tmps.take()
            FLT = TMP[:, iflt, :].rearrange("p (n w) -> p n w", n=2)
            FHL = mk("FHL", [P, 1152], F32R)
            CM = mk("CM", [P, 640])
            w_hop[0] = [8 + i for i in range(8)] + list(range(8)) + list(range(16, 32))
            pair = lambda b: b[:, :].rearrange("p (n w) -> p n w", n=2)
            tk = {}

            def proj(i):
                outs = wide(("in", l, i), 8, 256, NH, NL, tn)
                t_nread[0] = outs[1][2]
                return outs[0][0], outs[1][2]

            def plain(i, dst, name, scale=1.0):
                b, tm = proj(i)
                t = copy_a(dst, pair(b), tm, scale=scale)
                banks.give(b, t)
                tk[name] = t

            def turned(i, dst, name, scale):
                b, tm = proj(i)
                ta, te = rotate(dst, pair(b), tm, const_at("c2", 0, 256), const_at("s2", 0, 256), scale)
                banks.give(b, ta)
                tk[name] = te

            b, tm = proj(2)
            t = copy_a(KC[:, :, :], pair(b), tm)
            banks.give(b, t)
            tk["kc"] = t
            t_f = []
            tz = zero(FLT, t_flt)
            for kind in range(2):
                for par in range(2):
                    ps = slice(64 * par, 64 * par + 64)
                    src = bass.AP(KC[:, :, :].tensor, 64 * par * 512 + kind * 256 + par, [[512, 64], [2, 16], [16, 15]])
                    pos = SMALL[ps, SM["cpos"] + (2 * l + kind) * 16:SM["cpos"] + (2 * l + kind) * 16 + 16]
                    dst = FLT[ps, kind, :].rearrange("p (a n) -> p a n", a=16)[:, :, 0:15]
                    t_f.append(tt(dve, dst, src, pos.unsqueeze(2).to_broadcast([64, 16, 15]), ALU.add, tk["kc"], tz))
            fv = FHL[:, 0:1024].rearrange("p (c k s n) -> p c k s n", c=2, k=16, s=2)
            t_pad = zero(FHL[:, 1024:1152])
            t1 = []
            for kind in range(2):
                f = FLT[:, kind, :].rearrange("p (k n) -> p k n", k=16)
                t1.append((copy_a(fv[:, kind, :, 0, :], f, t_f), f))
            t_f = [t_pad]
            for kind, (t, f) in enumerate(t1):
                t_f.append(tt(dve, fv[:, kind, :, 1, :], f, fv[:, kind, :, 0, :].bitcast(F32), ALU.subtract, t))
            tmps.give(iflt, t_f)
            KCT = CM[:, 0:16]
            VCB = CM[:, 128:384]
            tz = zero(CM[:, 0:384])
            turned(0, QN[:, :, :], "qn", 0.125)
            turned(1, KN[:, :, :], "kn", 1.0)
            (b, tm), = tall(("in", l, 3), 144, 2, tn)
            t = copy_a(VN[:, :, :], pair(b)[:, :, 0:144], tm)
            banks.give(b, t)
            tk["vn"] = t
            i, tfree = tmps.take()
            z, az, ez, lz, mz = (TMP[:, i, 8 * a:8 * a + 8].rearrange("p (q h) -> p q h", q=2) for a in range(5))
            fb = small_at("foxb", 4 * l, 4).unsqueeze(1).to_broadcast([P, 2, 4])
            t1 = tt(dve, z, VN[:, :, 140:144], fb, ALU.add, tk["vn"], tfree, t_small)
            t2 = activ(az, z, ACT.Abs, t1)
            t3 = activ(ez, az, ACT.Exp, t2, scale=-1.0)
            t4 = activ(lz, ez, ACT.Ln, t3, bias=1.0)
            t5 = ts(mz, z, 0.0, None, ALU.min, None, t1)
            t0 = zero(LF[:, :, :])
            lfv = LF[:, :, :].rearrange("p q (r l s) -> p q r l s", r=2, l=2)
            mz2, lz2 = (a.rearrange("p q (l r) -> p q r l", l=2) for a in (mz, lz))
            t6 = [tt(dve, lfv[:, :, :, :, s], mz2, lz2, ALU.subtract, t4, t5, t0) for s in range(2)]
            tmps.give(i, t6)
            GS = CM[:, 512:536].rearrange("p (q g) -> p q g", q=2)
            t = activ(GS, VN[:, :, 128:140], ACT.Tanh, tk["vn"], scale=0.5)
            tk["gs"] = ts(GS, GS, 0.5, 0.5, ALU.mult, ALU.add, t)
            plain(5, QF[:, :, :], "qf", 0.125)
            plain(6, KF[:, :, :], "kf")
            b, free = banks.take()
            for q in range(2):
                tm = tr(b[:, q * P:q * P + P], LF[:, q, :], t6, free, signal=(q == 1))
            t = scan_sum(CR[:, :], const_at("ones", 0, 256), b[:, 0:256], tm)
            banks.give(b, t)
            first_, second, minus = (const_at("rows", a) for a in range(3))
            t = ts(NCR[:, :], CR[:, :], minus, first_, ALU.mult, ALU.add, t)
            tk["cr"] = ts(CR[:, :], CR[:, :], first_, second, ALU.mult, ALU.add, t)
            (b, tm), = tall(("in", l, 4), 256, 2, tn)
            t = copy_a(VF[:, :, :], pair(b), tm)
            banks.give(b, t)
            tk["vf"] = t
            def compress():
                rows = []
                for kind in range(2):
                    wh, wl, tw = W.take(("cmp", l, kind), 16, 128)
                    b, free = banks.take()
                    for k in range(16):
                        lhs = FHL[:, 512 * kind + 32 * k:512 * kind + 32 * k + P]
                        mm(b[:, 0:P], lhs, wh[:, k, :], k == 0, False, tw[k], t_f, free)
                        last = mm(b[:, 0:P], lhs, wl[:, k, :], False, k == 15, signal=(k == 15))
                    W.done(last)
                    i, tfree = tmps.take()
                    t = copy_a(TMP[0:32, i, 0:P], b[0:32, 0:P], last, tfree)
                    banks.give(b, t)
                    rows.append((i, t))
                yield
                b, free = banks.take()
                x, th, h2 = (CM[:, 544 + 32 * a:576 + 32 * a] for a in range(3))
                t1 = []
                for kind, (i, t) in enumerate(rows):
                    o = b[:, 16 * kind:16 * kind + 16]
                    tm = mm(o, TMP[0:32, i, 0:P], CONST[0:32, CO["sum16"]:CO["sum16"] + 16], True, True, t, free,
                            signal=True)
                    tmps.give(i, tm)
                for kind in range(2):
                    t1.append(ts(x[:, 16 * kind:16 * kind + 16], b[:, 16 * kind:16 * kind + 16],
                                 small_at("cb1", 2 * l + kind), None, ALU.add, None, tm))
                banks.give(b, t1[-1])
                t2 = activ(th, x, ACT.Tanh, t1, scale=0.5)
                t3 = stt(h2, th, 1.0, x, ALU.add, ALU.mult, t2)
                iv, tfree = tmps.take()
                hw = TMP[:, iv, 0:128].rearrange("p (h n) -> p h n", h=4)
                tz2 = zero(TMP[:, iv, 0:128], tfree)
                tv = copy_v(hw[:, :, 0:15], h2[:, 16:31].unsqueeze(1).to_broadcast([P, 4, 15]), t3, tz2)
                yield
                w2k = small_at("w2", (2 * l) * 128, 128)
                w2v = small_at("w2", (2 * l + 1) * 128, 64)
                b, free = banks.take()
                tm = mm(b[:, 0:16], w2k, h2[:, 0:16], True, True, t3, free, signal=True)
                i, tfree = tmps.take()
                kc, ks = TMP[:, i, 0:16], TMP[:, i, 16:32]
                t1 = ts(kc, b[:, 0:16], 0.5, small_at("cb2", l), ALU.mult, ALU.add, tm, tfree)
                banks.give(b, t1)
                t2 = shuffle(ks, kc, w_hop[0], t1)
                t3 = tt(dve, KCT, kc, const_at("cmpc", 0, 16), ALU.mult, t1, tz)
                t4 = tt(dve, ks, ks, const_at("cmps", 0, 16), ALU.mult, t2)
                t5 = tt(dve, KCT, KCT, ks, ALU.add, t3, t4)
                tmps.give(i, t5)
                tk["kct"] = t5
                b, free = banks.take()
                tm = mm(b[:, 0:64], TMP[:, iv, 0:128], w2v, True, True, tv, free, signal=True)
                tmps.give(iv, tm)
                tv4 = []
                for h in range(4):
                    ps = slice(32 * h, 32 * h + 15)
                    b2 = late_sb[0][ps, LATE["cb2v"] + 64 * l:LATE["cb2v"] + 64 * l + 64]
                    tv4.append(stt(VCB[ps, 64 * h:64 * h + 64], b[ps, 0:64], 0.5, b2, ALU.mult, ALU.add, tm, tz))
                banks.give(b, tv4[-1])
                tk["vcb"] = tv4

            oparts = {}

            def add_nsa(qt, v, r3, *w):
                o = ON[:, qt, :].rearrange("p (h d) -> p h d", h=4)
                if ("nsa", qt) not in oparts:
                    t = t0 = tt(dve, o, v, r3, ALU.mult, *w)
                else:
                    i, tfree = tmps.take()
                    x3 = TMP[:, i, 0:256].rearrange("p (h d) -> p h d", h=4)
                    t0 = tt(dve, x3, v, r3, ALU.mult, tfree, *w)
                    t = tt(dve, o, o, x3, ALU.add, t0, oparts["nsa", qt])
                    tmps.give(i, t)
                oparts["nsa", qt] = t
                return t0

            def attend_cmp(qt):
                st, sfree = stats.take()
                nm, sm, r = (STAT[:, st, 4 * a:4 * a + 4] for a in range(3))
                b, free = banks.take()
                s3 = b[:, 0:64].rearrange("p (h n) -> p h n", h=4)[:, :, 0:15]
                tm = None
                for h in (0, 2, 1, 3):
                    ps = slice(64 * (h % 2), 64 * (h % 2) + 64)
                    tm = mm(b[:, 16 * h:16 * h + 15], QN[ps, h // 2, qt * P:qt * P + P], KCT[ps, 0:15], True, True,
                            tk["qn"], tk["kct"], free, tm, signal=(h > 1))
                yield
                i, tfree = tmps.take()
                e3 = TMP[:, i, 0:128].rearrange("p (h n) -> p h n", h=4)
                tz = zero(TMP[:, i, 0:128], tfree)
                e15 = e3[:, :, 0:15]
                over = lambda name: const_at(name, 16 * qt, 15).unsqueeze(1).to_broadcast([P, 4, 15])
                t1 = tt(dve, s3, s3, over("cmpadd"), ALU.add, tm)
                t2 = reduce(nm, s3, ALU.max, True, t1, sfree)
                t3 = tt(dve, e15, s3, nm.unsqueeze(2).to_broadcast([P, 4, 15]), ALU.add, t2, tz)
                banks.give(b, t3)
                t4 = activ(e15, e15, ACT.Exp, t3)
                t5 = reduce(sm, e15, ALU.add, False, t4)
                t6 = recip(r, sm, t5)
                t7 = tt(dve, e15, e15, over("cmpmul"), ALU.mult, t5)
                t8 = tt(dve, e15, e15, r.unsqueeze(2).to_broadcast([P, 4, 15]), ALU.mult, t6, t7)
                stats.give(st, t8)
                yield
                b, free = banks.take()
                tm = tr(b[:, 0:P], TMP[:, i, 0:P], t8, free, signal=True)
                tmps.give(i, tm)
                j, jfree = tmps.take()
                te = copy_a(TMP[:, j, 0:P], b[:, 0:P], tm, jfree)
                banks.give(b, te)
                yield
                b, free = banks.take()
                tm = mm(b[:, 0:256], TMP[:, j, 0:P], VCB, True, True, te, tk["vcb"], free, signal=True)
                tmps.give(j, tm)
                g = GS[:, qt, 0:4].unsqueeze(2).to_broadcast([P, 4, 64])
                t = add_nsa(qt, b[:, 0:256].rearrange("p (h d) -> p h d", h=4), g, tm, tk["gs"])
                banks.give(b, t)

            def attend_causal(kind, qt):
                nk = P * (qt + 1)
                per = 512 // nk
                order_h = (0, 2, 1, 3)
                fox = kind == 2
                st, sfree = stats.take()
                nm, sm, r = (STAT[:, st, 4 * a:4 * a + 4] for a in range(3))
                nmr = nm.rearrange("p (l r) -> p r l", r=2)
                ptiles, sc = [], []
                for g in range(4 // per):
                    b, free = banks.take()
                    tm = None
                    for a in range(per):
                        h = order_h[g * per + a]
                        ps = slice(64 * (h % 2), 64 * (h % 2) + 64)
                        o = b[:, a * nk:a * nk + nk]
                        if fox:
                            q, k, tqk = QF[ps, h // 2, qt * P:qt * P + P], KF[ps, h // 2, 0:nk], [tk["qf"], tk["kf"]]
                        else:
                            q, k, tqk = QN[ps, h // 2, qt * P:qt * P + P], KN[ps, kind, 0:nk], [tk["qn"], tk["kn"]]
                        tm = mm(o, q, k, True, not fox, tqk, free, tm if a == 2 else None, signal=True)
                        if fox:
                            rw = slice(64 * (h % 2) + 32 * (h // 2), 64 * (h % 2) + 32 * (h // 2) + 2)
                            tm = mm(o, CR[rw, qt * P:qt * P + P], NCR[rw, 0:nk], False, True, tk["cr"], tm, signal=True)
                    sc.append((b, tm))
                yield
                for g, (b, tm) in enumerate(sc):
                    b3 = b[:, :].rearrange("p (a k) -> p a k", a=per)
                    dg = b3[:, :, nk - P:nk]
                    t1 = tt(dve, dg, dg, const_at("causal", 0, P).unsqueeze(1).to_broadcast([P, per, P]), ALU.add, tm)
                    if per == 4:
                        t2 = reduce(nmr, b[:, :].rearrange("p (r l k) -> p r l k", r=2, l=2), ALU.max, True, t1, sfree)
                    else:
                        t2 = reduce(nmr[:, g, :], b3, ALU.max, True, t1, sfree)
                    i, tfree = tmps.take()
                    for a in range(per):
                        h = order_h[g * per + a]
                        t3 = activ(TMP[:, i, a * nk:a * nk + nk], b[:, a * nk:a * nk + nk], ACT.Exp, t2, tfree,
                                   bias=nm[:, h:h + 1], accum_out=sm[:, h:h + 1])
                    banks.give(b, t3)
                    ptiles.append((i, t3))
                t4 = recip(r, sm, ptiles[-1][1], sfree)
                if kind < 2:
                    t4 = tt(dve, r, r, GS[:, qt, 4 + 4 * kind:8 + 4 * kind], ALU.mult, t4, tk["gs"])
                yield
                turned_ = []
                for i, t3 in ptiles:
                    b, free = banks.take()
                    for a in range(4):
                        tm = tr(b[:, a * P:a * P + P], TMP[:, i, a * P:a * P + P], t3, free, signal=(a == 3))
                    tmps.give(i, tm)
                    j, jfree = tmps.take()
                    te = copy_a(TMP[:, j, :], b[:, :], tm, jfree)
                    banks.give(b, te)
                    turned_.append((j, te))
                yield
                yield
                b, free = banks.take()
                for n, h in enumerate(order_h):
                    j, te = turned_[n // per]
                    for k in range(qt + 1):
                        c = ((n % per) * (qt + 1) + k) * P
                        v = VF[:, k, 64 * h:64 * h + 64] if kind == 2 else VN[:, k, 64 * kind:64 * kind + 64]
                        tm = mm(b[:, 64 * h:64 * h + 64], TMP[:, j, c:c + P], v, k == 0, k == qt, te,
                                tk["vf"] if kind == 2 else tk["vn"], free, signal=(k == qt and n % per == per - 1))
                    if n % per == per - 1:
                        tmps.give(j, tm)
                yield
                o = OF[:, qt, :].rearrange("p (h d) -> p h d", h=4)
                r3 = r.unsqueeze(2).to_broadcast([P, 4, 64])
                v3 = b[:, 0:256].rearrange("p (h d) -> p h d", h=4)
                if kind == 2:
                    t = tt(dve, o, v3, r3, ALU.mult, tm, t4)
                    banks.give(b, t)
                    oparts["fox", qt] = t
                else:
                    t = add_nsa(qt, v3, r3, tm, t4)
                    banks.give(b, t)
                stats.give(st, t)

            def gates(i):
                b, tm = proj(11 + i)
                j, tfree = tmps.take()
                t = activ(TMP[:, j, :], b[:, :], ACT.Tanh, tm, tfree, scale=0.5)
                g = G[:, 2 * i:2 * i + 2, :]
                t = stt(g, TMP[:, j, :].rearrange("p (n w) -> p n w", n=2), 1.0, pair(b), ALU.add, ALU.mult, t)
                banks.give(b, t)
                tmps.give(j, t)
                tk["g", i] = t

            order = (1, 2, 0, 3)
            m_free = [[], []]

            def merge(n_, j):
                b, tm = proj(15 + 4 * order[n_] + j)
                dst = M[:, n_ % 2, 2 * j:2 * j + 2, :]
                t = activ(dst, pair(b), ACT.Tanh, tm, m_free[n_ % 2], scale=0.5)
                banks.give(b, t)
                tk["m", order[n_], j] = t

            def gated(n, src, tsrc):
                i, tfree = tmps.take()
                zf = TMP[:, i, :].rearrange("p (n w) -> p n w", n=2)
                t1 = tt(dve, zf, src, G[:, 2 * n:2 * n + 2, :], ALU.mult, tsrc, tk["g", n], tfree)
                t2 = split_from(ZH[:, n, :, :], ZL[:, n, :, :], zf, None, 0.5, t1)
                tmps.give(i, t2)
                tk["z", n] = t2
                return t1

            def pooling():
                b, tm = proj(7)
                tz = zero_p(PU[:, :, :, 0:16])
                u0 = PU[:, 0, :, 16:272]
                t = copy_a(u0, pair(b), tm)
                banks.give(b, t)
                tz2 = [tz, t]
                cur = 0
                t_p = tz2

                def rows_of(s, c, sh, lo=0, hi=P):
                    return PU[lo:hi, s, c, 16 - sh:272 - sh]

                a = PU[:, 1, :, 16:272]
                t1 = tt(dve, a, PU[:, 0, :, 16:272], PU[:, 0, :, 15:271], ALU.add, t_p)
                i, f1 = tmps.take()
                S4 = TMP[:, i, :]
                ps = slice(64, 128)
                t4a = tt(dve, S4[ps, 0:256], PU[ps, 1, 0, 16:272], PU[ps, 1, 0, 14:270], ALU.add, t1, f1)
                w4 = PW[:, 0, :]
                w8 = PW[:, 1, :]
                t4b = tt(dve, w4[:, 16:272], PU[:, 1, 1, 16:272], PU[:, 1, 1, 14:270], ALU.add, t1, t_pw)
                t8 = tt(dve, w8[:, 16:272], w4[:, 16:272], w4[:, 12:268], ALU.add, t4b)
                t16 = tt(dve, S4[ps, 256:512], w8[ps, 16:272], w8[ps, 8:264], ALU.add, t8, f1)
                lo = slice(0, 64)
                tc1 = copy_v(S4[lo, 0:256], PU[lo, 1, 0, 16:272], t1, f1)
                tc2 = copy_v(S4[lo, 256:512], w8[lo, 16:272], t8, f1)
                t = tt(dve, S4, S4, const_at("icnt", 0, 512), ALU.mult, t4a, t16, tc1, tc2)
                s3 = S4.rearrange("p (n w) -> p n w", n=2)
                t = tt(dve, s3, s3, PU[:, 0, :, 16:272], ALU.subtract, t)
                pooled.append((i, S4, t))

            pooled = []

            def pool_out():
                i, S4, t = pooled.pop()
                b, free = banks.take()
                for c in range(2):
                    w = small_at("poolw", (2 * l + c) * 128, 128)
                    tm = mm(b[:, 256 * c:256 * c + 256], w, S4[:, 256 * c:256 * c + 256], True, True, t, free,
                            signal=(c == 1))
                i2, f2 = tmps.take()
                for c in range(2):
                    t = ts(TMP[:, i2, 256 * c:256 * c + 256], b[:, 256 * c:256 * c + 256],
                           small_at("pscale", 2 * l + c), None, ALU.mult, None, tm, f2)
                banks.give(b, t)
                tmps.give(i, tm)
                tg = gated(1, TMP[:, i2, :].rearrange("p (n w) -> p n w", n=2), t)
                tmps.give(i2, tg)

            PW = mk("PW", [P, 2, 272])
            t_pw = zero_p(PW[:, :, 0:16])


            def conv_in():
                b, tm = proj(8)
                i, tfree = tmps.take()
                t = copy_a(TMP[:, i, :], b[:, :], tm, tfree)
                banks.give(b, t)
                b, tm = proj(9)
                t2 = copy_a(CBG[:, :, :], pair(b), tm)
                banks.give(b, t2)
                tk["cbg"] = t2
                b, tm = proj(10)
                tz = zero_p(CXY[:, :, 0:2])
                x3 = TMP[:, i, :].rearrange("p (n w) -> p n w", n=2)
                t = tt(dve, CXY[:, :, 2:258], pair(b), x3, ALU.mult, t, tm)
                banks.give(b, t)
                tmps.give(i, t)
                j, tfree = tmps.take()
                y = TMP[:, j, :].rearrange("p (n w) -> p n w", n=2)
                for c in range(2):
                    w = lambda tap: small_at("cw", (3 * l + tap) * 2 + c)
                    q = ts(y[:, c, :], CXY[:, c, 0:256], w(0), None, ALU.mult, None, t, tz, tfree)
                    q = stt(y[:, c, :], CXY[:, c, 1:257], w(1), y[:, c, :], ALU.mult, ALU.add, q)
                    q = stt(y[:, c, :], CXY[:, c, 2:258], w(2), y[:, c, :], ALU.mult, ALU.add, q)
                q = tt(dve, y, y, CBG[:, :, :], ALU.mult, q, tk["cbg"])
                tg = gated(2, y, q)
                tmps.give(j, tg)

            def turn_out(name, n, src):
                b, free = banks.take()
                for c in range(2):
                    for q in range(2):
                        tm = tr(b[:, c * 256 + q * P:c * 256 + q * P + P], src[:, q, c * P:c * P + P],
                                oparts[name, 0], oparts[name, 1], free, signal=(c == 1 and q == 1))
                t = gated(n, pair(b), tm)
                banks.give(b, t)

            t_acc = {}
            ta = []

            def split_sum(mp):
                s = slice(2 * mp, 2 * mp + 2)
                a, nh, nl = ACC[:, s, :], NH[:, s, 0:256], NL[:, s, 0:256]
                t = copy_a(nh, a, t_acc[mp], t_nread[0])
                t = tt(pool if mp < 2 else dve, nl, a, nh.bitcast(F32), ALU.subtract, t)
                ta.extend([[t], [t]])

            def branch(n_):
                n = order[n_]
                wh, wl, tw = W.take(("br", l, n), 2, 1024)
                read = []
                for mp in range(4):
                    b, free = banks.take()
                    for j in range(2):
                        m = 2 * mp + j
                        for k in range(2):
                            last = mm3(b[:, 256 * j:256 * j + 256], wh[:, k, m * P:m * P + P], wl[:, k, m * P:m * P + P],
                                       ZH[:, n, k, :], ZL[:, n, k, :], k == 0, k == 1, tw[k], tk["z", n], free,
                                       signal=(j == 1 and k == 1))
                    msl = M[:, n_ % 2, 2 * mp:2 * mp + 2, :]
                    a = ACC[:, 2 * mp:2 * mp + 2, :]
                    if n_ == 0:
                        t = stt(a, msl, 1.0, pair(b), ALU.add, ALU.mult, last, tk["m", n, mp])
                        banks.give(b, t)
                        read.append(t)
                    else:
                        i, tfree = tmps.take()
                        x = TMP[:, i, :].rearrange("p (n w) -> p n w", n=2)
                        t = stt(x, msl, 1.0, pair(b), ALU.add, ALU.mult, last, tk["m", n, mp], tfree)
                        banks.give(b, t)
                        read.append(t)
                        t = tt(dve if n_ == 3 else pool, a, a, x, ALU.add, t, t_acc[mp])
                        tmps.give(i, t)
                    t_acc[mp] = t
                    if n_ == 3 and mp:
                        split_sum(mp - 1)
                W.done(last)
                m_free[n_ % 2] = read

            fl = [lambda i=i: gates(i) for i in (1, 2, 0, 3)]
            fl += [pooling, conv_in, pool_out]
            for n_ in range(2):
                fl += [lambda n_=n_, j=j: merge(n_, j) for j in range(4)]
            fl += [lambda n_=n_: branch(n_) for n_ in range(2)]
            jobs = [compress()] + [attend_causal(k, q) for k in (2, 0) for q in range(2)]
            jobs += [attend_causal(1, q) for q in range(2)] + [attend_cmp(0), attend_cmp(1)]
            run_jobs(jobs, fl)
            turn_out("nsa", 0, ON)
            for j in range(4):
                merge(2, j)
            turn_out("fox", 3, OF)
            branch(2)
            for j in range(4):
                merge(3, j)
            branch(3)
            split_sum(3)
            R = Rms(256)
            for i in range(4):
                outs = wide(("out", l, i), 8, 256, NH, NL, ta)
                R.sums()
                x = X[:, 2 * i:2 * i + 2, 0:256]
                t = stt(x, pair(outs[0][0]), 0.5, x, ALU.mult, ALU.add, outs[1][2], t_xt[2 * i], t_xt[2 * i + 1])
                banks.give(outs[0][0], t)
                t_xt[2 * i] = t_xt[2 * i + 1] = [t]
                R.square(2 * i + 2)
            t_nread[0] = outs[1][2]
            stack.close()

        gain_in_place("fng", R)
        W.loads()
        assert sorted(W.keys) == sorted(KEYS) and len(W.used) == len(KEYS)
        for m in range(DT):
            t_out = sp.dma(lambda e, m=m: e.dma_start(out[:, m, :], X[:, m, 0:256]), d_out, t_xt[m])
        end = t_out

        block = ctx.enter_context(nc.Block())

        @block.sync
        def _(e):
            sp.play(e)
            e.wait_ge(*end)

        @block.scalar
        def _(e):
            act.play(e)

        @block.vector
        def _(e):
            dve.play(e)

        @block.gpsimd
        def _(e):
            pool.play(e)

        @block.tensor
        def _(e):
            pe.play(e)




def pack_weights(v):
    w = np.zeros((len(KEYS), P, UNIT), np.float32)

    def put(n, a, nk):
        a = a.reshape(nk, P, a.shape[1]).transpose(1, 0, 2).reshape(P, -1)
        w[n, :, :a.shape[1]] = a

    for n, key in enumerate(KEYS):
        kind, l = key[0], key[1]
        if kind == "ada":
            _, _, g, half = key
            put(n, v["ada_w"][l, 512 * half:512 * half + 512, 512 * g:512 * g + 512], 4)
        elif kind == "qkv":
            put(n, v["a_wqkv" if l == 0 else "b_wqkv"][0, :, 256 * key[2]:256 * key[2] + 256], 8)
        elif kind == "wo":
            put(n, v["a_wo" if l == 0 else "b_wo"][0, :, 256 * key[2]:256 * key[2] + 256], 8)
        elif kind == "up":
            j = key[2]
            u = v["ffn_up"][l]
            put(n, np.concatenate([u[:, P * j:P * j + P], u[:, FF + P * j:FF + P * j + P]], 1), 8)
        elif kind == "down":
            _, _, c, m = key
            put(n, v["ffn_down"][l, 1408 * c:1408 * c + 1408, P * m:P * m + P], 11)
        elif kind == "in":
            cols = in_columns(key[2])
            if key[2] == 3:
                put(n, v["w_in_2"][l][:, cols[:144]], 8)
            else:
                put(n, v["w_in_2"][l][:, cols], 8)
        elif kind == "cmp":
            put(n, v["cmp_w1_2"][l, key[2]], 16)
        elif kind == "br":
            put(n, v["w_branch_2"][l, key[2]], 2)
        elif kind == "out":
            put(n, v["w_out_2"][l, :, 256 * key[2]:256 * key[2] + 256], 8)
    return w


def pack_small(v, late):
    s = np.zeros((P, NSM), np.float32)

    def put(name, a, off=0):
        to, at = (late, LATE) if name in LATE else (s, SM)
        to[:a.shape[0], at[name] + off:at[name] + off + a.shape[1]] = a

    cols = lambda a: np.asarray(a).reshape(-1, P).T
    put("c", cols(v["c"]))
    put("cc", cols(v["c_ctx"]))
    put("adab", cols(v["ada_b"]))
    put("nmix", cols(v["norm_mix"]))
    put("nffn", cols(v["norm_ffn"]))
    put("nout", cols(v["norm_out"]))
    put("fconv", cols(v["ffn_conv"]))
    put("fconvb", cols(v["ffn_conv_b"]))
    put("subln", cols(v["a_subln"]))
    put("normg", cols(v["norm_g_2"]))
    put("foxb", np.tile(v["fox_f_bias_2"].reshape(1, 8), (P, 1)))
    put("cpos", v["cmp_pos_2"].reshape(4, 16, P).transpose(2, 0, 1).reshape(P, 64))
    put("cb1", cols(v["cmp_b1_2"]))
    for l in range(2):
        put("cb2", np.tile(v["cmp_b2_2"][l, 0].reshape(64, 1), (2, 1)), l)
        put("cb2v", np.tile(v["cmp_b2_2"][l, 1].reshape(1, 64), (P, 1)), 64 * l)
        put("w2", np.tile(v["cmp_w2_2"][l, 0], (1, 2)), 2 * l * 128)
        put("w2", v["cmp_w2_2"][l, 1], (2 * l + 1) * 128)
        for c in range(2):
            for g in range(2):
                o = LATE["poolw"] + (2 * l + c) * 128
                late[64 * g:64 * g + 64, o + 64 * g:o + 64 * g + 64] = v["pool_w_2"][l, 2 * c + g]
    put("pscale", cols(v["pool_scale_2"]))
    put("cw", cols(v["conv_w_2"]))
    put("fng", cols(v["final_norm_g_2"]))
    put("lam", np.tile(v["a_lambda"].reshape(1, 256), (P, 1)))
    return s


def pack_rpb(v):
    b = v["b_rpb"][0]
    rows = np.stack([b[:, 7 - r:11 - r, ::-1] for r in range(4)])
    flat = np.zeros(64 + rows.size + 64, np.float32)
    flat[64:64 + rows.size] = rows.ravel()
    return flat


def layout(inputs):
    v = {k: np.asarray(a) for k, a in inputs.items()}
    consts, late = constants()
    small = pack_small(v, late)
    x = np.concatenate([v["x"][0], v["ctx"][0]], 0).T.reshape(DT, P, 512).transpose(1, 0, 2)
    return {
        "wstream": pack_weights(v),
        "small": small,
        "consts": consts,
        "late": late,
        "rpb": pack_rpb(v),
        "xin": np.ascontiguousarray(x),
    }


def kernel(**inputs):
    import concourse.bacc as _bacc
    from concourse.bass_utils import run_bass_kernel_spmd as _run

    arrays = layout(inputs)
    nc = _bacc.Bacc("TRN2", target_bir_lowering=False, num_devices=1, dynamic_dma_scratch_size=1024)
    args = [nc.dram_tensor(n, a.shape, F32, kind="ExternalInput").ap() for n, a in arrays.items()]
    args.append(nc.dram_tensor("out", (P, DT, 256), F32, kind="ExternalOutput").ap())
    bass_two_block_decoder(nc, *args)
    r = _run(nc, [arrays], core_ids=[0])
    got = r.results[0]["out"]
    return np.ascontiguousarray(got.transpose(2, 1, 0)).reshape(1, 256, D)
```
